# Optimizing a Trainium2 kernel written in Bass

```python
import math
import jax
import jax.numpy as jnp
from jax import lax
import numpy as np

D_MODEL = 1024
BATCH = 1
SEQ = 512
DEPTH = 2
DEC_BATCH = 8
DEC_SEQ = 8
PAST_LEN = 2048
PAGE_SIZE = 128

N_EVEN = (DEPTH + 1) // 2
N_ODD = DEPTH // 2
HEAD_DIM = 64
H_DIFF = D_MODEL // 256
DV_DIFF = 2 * HEAD_DIM
H_DIL = D_MODEL // 128
ROT_DIM = HEAD_DIM // 4
ROPE_THETA = 500000.0
DIL_PATTERNS = ((128, 1), (512, 4), (2048, 16))
WIN_MAX = 2048
CONV_K = 31
D_CONV = D_MODEL
N_GROUPS = 4
E_PER_GROUP = 8
N_EXPERTS = N_GROUPS * E_PER_GROUP
TOP_K_INNER = 2
D_EXPERT = D_MODEL // 2
Q_BLOCK = 128
MOE_BLOCK = 128
EPS = 1e-6
NEG = -1e30
D_QK_DIFF = H_DIFF * HEAD_DIM
D_V_DIFF = H_DIFF * DV_DIFF
D_DIL = H_DIL * HEAD_DIM
D_PROJ = 4 * D_QK_DIFF + D_V_DIFF + 3 * D_DIL
D_MIX = D_V_DIFF + D_DIL

kernel_name = "hybrid_diffattn_dilated_conformer_hmoe_step"

def rmsnorm(x, g):
    xf = x.astype(jnp.float32)
    y = xf * lax.rsqrt(jnp.mean(xf * xf, axis=-1, keepdims=True) + EPS) * g.astype(jnp.float32)
    return y.astype(x.dtype)

def layernorm(x, g, b):
    xf = x.astype(jnp.float32)
    mu = jnp.mean(xf, axis=-1, keepdims=True)
    xc = xf - mu
    var = jnp.mean(xc * xc, axis=-1, keepdims=True)
    y = xc * lax.rsqrt(var + EPS) * g.astype(jnp.float32) + b.astype(jnp.float32)
    return y.astype(x.dtype)

def rope(x, pos):
    half = ROT_DIM // 2
    inv = ROPE_THETA ** (-jnp.arange(half, dtype=jnp.float32) / half)
    ang = pos.astype(jnp.float32)[:, None] * inv[None, :]
    cos = jnp.cos(ang)[:, None, :]
    sin = jnp.sin(ang)[:, None, :]
    xr = x[..., :ROT_DIM].astype(jnp.float32)
    x1, x2 = xr[..., :half], xr[..., half:]
    rot = jnp.concatenate([x1 * cos - x2 * sin, x2 * cos + x1 * sin], axis=-1)
    return jnp.concatenate([rot.astype(x.dtype), x[..., ROT_DIM:]], axis=-1)

def even_project(h, w_in, pos):
    z = h @ w_in
    a = D_QK_DIFF
    cuts = [a, 2 * a, 3 * a, 4 * a, 4 * a + D_V_DIFF, 4 * a + D_V_DIFF + D_DIL, 4 * a + D_V_DIFF + 2 * D_DIL]
    q1, q2, k1, k2, va, qb, kb, vb = jnp.split(z, cuts, axis=-1)
    lead = h.shape[:-1]
    hd = lambda t, n, d: t.reshape(*lead, n, d)
    q1 = rope(hd(q1, H_DIFF, HEAD_DIM), pos)
    q2 = rope(hd(q2, H_DIFF, HEAD_DIM), pos)
    k1 = rope(hd(k1, H_DIFF, HEAD_DIM), pos)
    k2 = rope(hd(k2, H_DIFF, HEAD_DIM), pos)
    va = hd(va, H_DIFF, DV_DIFF)
    qb = rope(hd(qb, H_DIL, HEAD_DIM), pos)
    kb = rope(hd(kb, H_DIL, HEAD_DIM), pos)
    vb = hd(vb, H_DIL, HEAD_DIM)
    return q1, q2, k1, k2, va, qb, kb, vb

def diff_core(q1, q2, k1, k2, v, lam, q_pos, k_pos):
    scale = HEAD_DIM ** -0.5
    mask = (k_pos[None, :] <= q_pos[:, None])[None, None]
    s1 = jnp.einsum('bqhd,bkhd->bhqk', q1, k1).astype(jnp.float32) * scale
    s2 = jnp.einsum('bqhd,bkhd->bhqk', q2, k2).astype(jnp.float32) * scale
    p1 = jax.nn.softmax(jnp.where(mask, s1, NEG), axis=-1)
    p2 = jax.nn.softmax(jnp.where(mask, s2, NEG), axis=-1)
    p = (p1 - lam * p2).astype(v.dtype)
    return jnp.einsum('bhqk,bkhd->bqhd', p, v)

def diff_attention_prompt(q1, q2, k1, k2, v, lam):
    b, s_len, h, d = q1.shape
    nb = s_len // Q_BLOCK
    k_pos = jnp.arange(s_len)

    def to_blocks(t):
        return t.reshape(b, nb, Q_BLOCK, h, d).transpose(1, 0, 2, 3, 4)

    def run(args):
        qa, qc, bi = args
        q_pos = bi * Q_BLOCK + jnp.arange(Q_BLOCK)
        return diff_core(qa, qc, k1, k2, v, lam, q_pos, k_pos)

    o = lax.map(run, (to_blocks(q1), to_blocks(q2), jnp.arange(nb)))
    return o.transpose(1, 0, 2, 3, 4).reshape(b, s_len, h, v.shape[-1])

def masked_softmax_lse(s, mask):
    s = jnp.where(mask, s, NEG)
    m = jnp.max(s, axis=-1, keepdims=True)
    e = jnp.exp(s - m)
    l = jnp.sum(e, axis=-1, keepdims=True)
    return e / l, (m + jnp.log(l))[..., 0]

def dilated_branch_prompt(q, k, v, window, dil):
    b, s_len, h, dh = q.shape
    n_back = window // dil
    blk = n_back
    span = dil * blk
    length = -(-s_len // span) * span
    pad = length - s_len
    nb = length // span
    scale = dh ** -0.5

    def blocks(t):
        t = jnp.pad(t, ((0, 0), (pad, 0), (0, 0), (0, 0)))
        t = t.reshape(b, length // dil, dil, h, dh).transpose(0, 2, 1, 3, 4)
        return t.reshape(b, dil, nb, blk, h, dh)

    def with_prev(t, axis):
        pw = [(0, 0)] * t.ndim
        pw[axis] = (1, 0)
        prev = lax.slice_in_dim(jnp.pad(t, pw), 0, nb, axis=axis)
        return jnp.concatenate([prev, t], axis=axis + 1)

    qb = blocks(q)
    kb = with_prev(blocks(k), 2)
    vb = with_prev(blocks(v), 2)
    valid = (jnp.arange(length) >= pad).reshape(length // dil, dil).T.reshape(dil, nb, blk)
    kvalid = with_prev(valid, 1)
    rel = (jnp.arange(blk)[:, None] + blk) - jnp.arange(2 * blk)[None, :]
    band = (rel >= 0) & (rel <= n_back)
    mask = band[None, None] & kvalid[:, :, None, :]
    s = jnp.einsum('brnqhd,brnkhd->brnhqk', qb, kb).astype(jnp.float32) * scale
    p, lse = masked_softmax_lse(s, mask[None, :, :, None])
    o = jnp.einsum('brnhqk,brnkhd->brnqhd', p.astype(v.dtype), vb)
    o = o.reshape(b, dil, length // dil, h, dh).transpose(0, 2, 1, 3, 4).reshape(b, length, h, dh)[:, pad:]
    lse = lse.transpose(0, 1, 2, 4, 3).reshape(b, dil, length // dil, h)
    lse = lse.transpose(0, 2, 1, 3).reshape(b, length, h)[:, pad:]
    return o, lse

def dilated_branch_sample(q, kc, vc, window, dil):
    n_new = q.shape[1]
    w = kc.shape[1] - n_new
    n_back = window // dil
    idx = w + jnp.arange(n_new)[:, None] - dil * jnp.arange(n_back + 1)[None, :]
    valid = idx >= 0
    idx = jnp.maximum(idx, 0)
    kg = kc[:, idx]
    vg = vc[:, idx]
    s = jnp.einsum('bqhd,bqkhd->bhqk', q, kg).astype(jnp.float32) * (q.shape[-1] ** -0.5)
    p, lse = masked_softmax_lse(s, valid[None, None])
    o = jnp.einsum('bhqk,bqkhd->bqhd', p.astype(vc.dtype), vg)
    return o, lse.transpose(0, 2, 1)

def merge_by_denominator(branches):
    outs = jnp.stack([o for o, _ in branches], axis=0)
    lses = jnp.stack([l for _, l in branches], axis=0)
    wts = jax.nn.softmax(lses, axis=0)[..., None].astype(outs.dtype)
    return jnp.sum(wts * outs, axis=0)

def even_merge(oa, ob, subln_gain, lam_init, w_out):
    lead = oa.shape[:-2]
    oa = rmsnorm(oa, subln_gain) * (1.0 - lam_init)
    cat = jnp.concatenate([oa.reshape(*lead, D_V_DIFF), ob.reshape(*lead, D_DIL)], axis=-1)
    return cat @ w_out

def conv_glu(h, w_pw1, b_pw1):
    u = h @ w_pw1 + b_pw1
    a, g = jnp.split(u, 2, axis=-1)
    return a * jax.nn.sigmoid(g)

def conv_rest(u_ext, w_dw, b_dw, ln_g, ln_b, w_pw2, b_pw2):
    c = lax.conv_general_dilated(u_ext, w_dw[:, None, :], window_strides=(1,), padding='VALID',
                                 dimension_numbers=('NWC', 'WIO', 'NWC'),
                                 feature_group_count=D_CONV) + b_dw
    c = layernorm(c, ln_g, ln_b)
    return jax.nn.silu(c) @ w_pw2 + b_pw2

def expert_dispatch(t, ids, wts, w_gate, w_up, w_down):
    n_tok, d = t.shape
    k = ids.shape[1]
    n_as = n_tok * k
    flat_e = ids.reshape(-1)
    flat_tok = jnp.repeat(jnp.arange(n_tok, dtype=jnp.int32), k)
    flat_w = wts.reshape(-1)
    order = jnp.argsort(flat_e)
    e_s, tok_s, w_s = flat_e[order], flat_tok[order], flat_w[order]
    counts = jnp.bincount(flat_e, length=N_EXPERTS)
    padded = (counts + MOE_BLOCK - 1) // MOE_BLOCK * MOE_BLOCK
    starts = jnp.cumsum(counts) - counts
    pstarts = jnp.cumsum(padded) - padded
    dest = pstarts[e_s] + jnp.arange(n_as, dtype=jnp.int32) - starts[e_s]
    n_blk = -(-n_as // MOE_BLOCK) + N_EXPERTS
    cap = n_blk * MOE_BLOCK
    slot_tok = jnp.zeros((cap,), jnp.int32).at[dest].set(tok_s)
    slot_w = jnp.zeros((cap,), t.dtype).at[dest].set(w_s)
    blk_expert = jnp.minimum(
        jnp.searchsorted(jnp.cumsum(padded), jnp.arange(n_blk) * MOE_BLOCK, side='right'),
        N_EXPERTS - 1)

    def run(args):
        tok, wb, e = args
        xb = t[tok]
        hb = jax.nn.silu(xb @ w_gate[e]) * (xb @ w_up[e])
        return (hb @ w_down[e]) * wb[:, None]

    y = lax.map(run, (slot_tok.reshape(n_blk, MOE_BLOCK), slot_w.reshape(n_blk, MOE_BLOCK), blk_expert))
    return jnp.zeros_like(t).at[slot_tok].add(y.reshape(cap, d))

def hier_moe(x, w_rg, w_re, w_g, w_u, w_d):
    shp = x.shape
    t = x.reshape(-1, shp[-1])
    g_logit = (t @ w_rg).astype(jnp.float32)
    g_prob = jax.nn.softmax(g_logit, axis=-1)
    g_idx = jnp.argmax(g_logit, axis=-1).astype(jnp.int32)
    g_w = jnp.take_along_axis(g_prob, g_idx[:, None], axis=1)
    e_logit = jnp.einsum('td,gde->tge', t, w_re).astype(jnp.float32)
    e_logit = jnp.take_along_axis(e_logit, g_idx[:, None, None], axis=1)[:, 0]
    e_prob = jax.nn.softmax(e_logit, axis=-1)
    top_w, top_i = lax.top_k(e_prob, TOP_K_INNER)
    top_w = top_w / jnp.sum(top_w, axis=-1, keepdims=True)
    ids = g_idx[:, None] * E_PER_GROUP + top_i.astype(jnp.int32)
    wts = (g_w * top_w).astype(x.dtype)
    return expert_dispatch(t, ids, wts, w_g, w_u, w_d).reshape(shp)

def setup_inputs(seed: int = 0) -> dict:
    key = jax.random.key(seed)
    ks = jax.random.split(key, 32)
    f32 = jnp.float32
    n_pages = PAST_LEN // PAGE_SIZE
    n_used = DEC_BATCH * n_pages
    n_phys = n_used + n_used // 4
    win_buf = min(WIN_MAX, PAST_LEN)

    def nrm(k, shape, scale=1.0):
        return jax.random.normal(k, shape, f32) * scale

    page_table = jax.random.permutation(ks[7], n_phys)[:n_used].reshape(DEC_BATCH, n_pages).astype(jnp.int32)
    return {
        "x_prompt": nrm(ks[0], (BATCH, SEQ, D_MODEL)),
        "x_sample": nrm(ks[1], (DEC_BATCH, DEC_SEQ, D_MODEL)),
        "cache_k_diff": nrm(ks[2], (N_EVEN, n_phys, PAGE_SIZE, H_DIFF, 2 * HEAD_DIM)),
        "cache_v_diff": nrm(ks[3], (N_EVEN, n_phys, PAGE_SIZE, H_DIFF, DV_DIFF)),
        "cache_win_k": nrm(ks[4], (N_EVEN, DEC_BATCH, win_buf, H_DIL, HEAD_DIM)),
        "cache_win_v": nrm(ks[5], (N_EVEN, DEC_BATCH, win_buf, H_DIL, HEAD_DIM)),
        "state_conv": nrm(ks[6], (N_ODD, DEC_BATCH, CONV_K - 1, D_CONV)),
        "page_table": page_table,
        "norm_mix": 1.0 + nrm(ks[8], (DEPTH, D_MODEL), 0.02),
        "norm_ffn": 1.0 + nrm(ks[9], (DEPTH, D_MODEL), 0.02),
        "norm_final": 1.0 + nrm(ks[10], (D_MODEL,), 0.02),
        "w_in_attn": nrm(ks[11], (N_EVEN, D_MODEL, D_PROJ), D_MODEL ** -0.5),
        "lambda_q1": nrm(ks[12], (N_EVEN, HEAD_DIM), 0.1),
        "lambda_k1": nrm(ks[13], (N_EVEN, HEAD_DIM), 0.1),
        "lambda_q2": nrm(ks[14], (N_EVEN, HEAD_DIM), 0.1),
        "lambda_k2": nrm(ks[15], (N_EVEN, HEAD_DIM), 0.1),
        "subln_gain": 1.0 + nrm(ks[16], (N_EVEN, DV_DIFF), 0.02),
        "w_out_attn": nrm(ks[17], (N_EVEN, D_MIX, D_MODEL), D_MIX ** -0.5),
        "w_pw1": nrm(ks[18], (N_ODD, D_MODEL, 2 * D_CONV), D_MODEL ** -0.5),
        "b_pw1": nrm(ks[19], (N_ODD, 2 * D_CONV), 0.02),
        "w_dw": nrm(ks[20], (N_ODD, CONV_K, D_CONV), CONV_K ** -0.5),
        "b_dw": nrm(ks[21], (N_ODD, D_CONV), 0.02),
        "ln_conv_gain": 1.0 + nrm(ks[22], (N_ODD, D_CONV), 0.02),
        "ln_conv_bias": nrm(ks[23], (N_ODD, D_CONV), 0.02),
        "w_pw2": nrm(ks[24], (N_ODD, D_CONV, D_MODEL), D_CONV ** -0.5),
        "b_pw2": nrm(ks[25], (N_ODD, D_MODEL), 0.02),
        "w_router_group": nrm(ks[26], (DEPTH, D_MODEL, N_GROUPS), D_MODEL ** -0.5),
        "w_router_expert": nrm(ks[27], (DEPTH, N_GROUPS, D_MODEL, E_PER_GROUP), D_MODEL ** -0.5),
        "w_exp_gate": nrm(ks[28], (DEPTH, N_EXPERTS, D_MODEL, D_EXPERT), D_MODEL ** -0.5),
        "w_exp_up": nrm(ks[29], (DEPTH, N_EXPERTS, D_MODEL, D_EXPERT), D_MODEL ** -0.5),
        "w_exp_down": nrm(ks[30], (DEPTH, N_EXPERTS, D_EXPERT, D_MODEL), D_EXPERT ** -0.5),
    }

def reference(x_prompt, x_sample, cache_k_diff, cache_v_diff, cache_win_k, cache_win_v, state_conv,
              page_table, norm_mix, norm_ffn, norm_final, w_in_attn, lambda_q1, lambda_k1, lambda_q2,
              lambda_k2, subln_gain, w_out_attn, w_pw1, b_pw1, w_dw, b_dw, ln_conv_gain, ln_conv_bias,
              w_pw2, b_pw2, w_router_group, w_router_expert, w_exp_gate, w_exp_up, w_exp_down):
    s_len = x_prompt.shape[1]
    n_dec, n_new = x_sample.shape[0], x_sample.shape[1]
    past = page_table.shape[1] * cache_k_diff.shape[2]
    pos_p = jnp.arange(s_len)
    pos_s = past + jnp.arange(n_new)
    k_pos_s = jnp.arange(past + n_new)
    xp, xs = x_prompt, x_sample
    kd_p, vd_p, kd_s, vd_s = [], [], [], []
    wk_p, wv_p, wk_s, wv_s = [], [], [], []
    cv_p, cv_s = [], []

    for l in range(DEPTH):
        i = l // 2
        hp = rmsnorm(xp, norm_mix[l])
        hs = rmsnorm(xs, norm_mix[l])
        if l % 2 == 0:
            lam_init = 0.8 - 0.6 * math.exp(-0.3 * l)
            lam = (jnp.exp(jnp.sum(lambda_q1[i].astype(jnp.float32) * lambda_k1[i].astype(jnp.float32)))
                   - jnp.exp(jnp.sum(lambda_q2[i].astype(jnp.float32) * lambda_k2[i].astype(jnp.float32)))
                   + lam_init)
            q1, q2, k1, k2, va, qb, kb, vb = even_project(hp, w_in_attn[i], pos_p)
            oa = diff_attention_prompt(q1, q2, k1, k2, va, lam)
            ob = merge_by_denominator([dilated_branch_prompt(qb, kb, vb, w, d) for (w, d) in DIL_PATTERNS])
            yp = even_merge(oa, ob, subln_gain[i], lam_init, w_out_attn[i])
            kd_p.append(jnp.concatenate([k1, k2], axis=-1))
            vd_p.append(va)
            n_keep = min(WIN_MAX, s_len)
            wk_p.append(kb[:, s_len - n_keep:])
            wv_p.append(vb[:, s_len - n_keep:])
            q1, q2, k1, k2, va, qb, kb, vb = even_project(hs, w_in_attn[i], pos_s)
            kd_new = jnp.concatenate([k1, k2], axis=-1)
            k_all = jnp.concatenate(
                [cache_k_diff[i][page_table].reshape(n_dec, past, H_DIFF, 2 * HEAD_DIM), kd_new], axis=1)
            v_all = jnp.concatenate(
                [cache_v_diff[i][page_table].reshape(n_dec, past, H_DIFF, DV_DIFF), va], axis=1)
            oa = diff_core(q1, q2, k_all[..., :HEAD_DIM], k_all[..., HEAD_DIM:], v_all, lam, pos_s, k_pos_s)
            kc = jnp.concatenate([cache_win_k[i], kb], axis=1)
            vc = jnp.concatenate([cache_win_v[i], vb], axis=1)
            ob = merge_by_denominator([dilated_branch_sample(qb, kc, vc, w, d) for (w, d) in DIL_PATTERNS])
            ys = even_merge(oa, ob, subln_gain[i], lam_init, w_out_attn[i])
            kd_s.append(kd_new)
            vd_s.append(va)
            wk_s.append(kc[:, n_new:])
            wv_s.append(vc[:, n_new:])
        else:
            up = conv_glu(hp, w_pw1[i], b_pw1[i])
            u_ext = jnp.pad(up, ((0, 0), (CONV_K - 1, 0), (0, 0)))
            yp = conv_rest(u_ext, w_dw[i], b_dw[i], ln_conv_gain[i], ln_conv_bias[i], w_pw2[i], b_pw2[i])
            cv_p.append(up[:, s_len - (CONV_K - 1):])
            us = conv_glu(hs, w_pw1[i], b_pw1[i])
            u_ext_s = jnp.concatenate([state_conv[i], us], axis=1)
            ys = conv_rest(u_ext_s, w_dw[i], b_dw[i], ln_conv_gain[i], ln_conv_bias[i], w_pw2[i], b_pw2[i])
            cv_s.append(u_ext_s[:, n_new:])
        xp = xp + yp
        xs = xs + ys
        xp = xp + hier_moe(rmsnorm(xp, norm_ffn[l]), w_router_group[l], w_router_expert[l],
                           w_exp_gate[l], w_exp_up[l], w_exp_down[l])
        xs = xs + hier_moe(rmsnorm(xs, norm_ffn[l]), w_router_group[l], w_router_expert[l],
                           w_exp_gate[l], w_exp_up[l], w_exp_down[l])

    y_prompt = rmsnorm(xp, norm_final)
    y_sample = rmsnorm(xs, norm_final)
    new_k_diff_prompt = jnp.stack(kd_p)
    new_v_diff_prompt = jnp.stack(vd_p)
    new_k_diff_sample = jnp.stack(kd_s)
    new_v_diff_sample = jnp.stack(vd_s)
    new_win_k_prompt = jnp.stack(wk_p)
    new_win_v_prompt = jnp.stack(wv_p)
    new_win_k_sample = jnp.stack(wk_s)
    new_win_v_sample = jnp.stack(wv_s)
    new_conv_prompt = jnp.stack(cv_p)
    new_conv_sample = jnp.stack(cv_s)
    return (y_prompt, y_sample, new_k_diff_prompt, new_v_diff_prompt, new_k_diff_sample, new_v_diff_sample,
            new_win_k_prompt, new_win_v_prompt, new_win_k_sample, new_win_v_sample,
            new_conv_prompt, new_conv_sample)


_drawn_inputs = setup_inputs


def setup_inputs(seed=0):
    import zlib

    import numpy as np

    out = dict(_drawn_inputs(seed))
    spreads = {}
    factors = {'norm_final': 2.911, 'b_pw1': 2.683}
    for name, (base, spread) in spreads.items():
        noise = np.random.default_rng([zlib.crc32(name.encode()), seed]).standard_normal(out[name].shape)
        drawn = base * np.exp(spread * noise) if base else spread * noise
        out[name] = jnp.asarray(drawn.astype(out[name].dtype))
    for name, factor in factors.items():
        out[name] = (out[name] * factor).astype(out[name].dtype)
    return out
```

```python
import math
from contextlib import ExitStack

import numpy as np
import concourse.bass as bass
from concourse import mybir

P = 128
D = 1024
KC = D // P
TP, TS = 512, 64
T = TP + TS
NT = 5
NB, NQ = 8, 8
PAST, PAGE = 2048, 128
NPG = PAST // PAGE
HD = 64
HA = 4
NEG = -1e30
EPS = 1e-6
SCALE = HD ** -0.5
LAM_INIT = 0.8 - 0.6 * math.exp(-0.3 * 0)
PATTERNS = ((128, 1), (512, 4), (2048, 16))
NE, F = 32, 512
NX = 8
CK = 31
NWIN = 1280
UE = CK - 1 + TP + NB * (CK - 1 + NQ)
FAR = 4.0e6
HALF = T // 2


def rows(t):
    return P if t < 4 else TS


def log_count(dist):
    dist = np.asarray(dist)
    n = sum(((dist >= 0) & (dist % d == 0) & (dist <= w)).astype(np.float32) for w, d in PATTERNS)
    return np.where(n > 0, np.log(np.maximum(n, 1)), NEG).astype(np.float32)


def constants():
    f = np.float32
    c = {}
    r, k = np.arange(P)[:, None], np.arange(P)[None, :]
    c["ident"] = np.eye(P, dtype=f)
    c["ones"] = np.ones((P, P), f)
    c["before"] = (r < k).astype(f)
    c["causal"] = np.where(k <= r, 0, NEG).astype(f)
    c["dilated"] = np.concatenate([log_count(P * d + r - k) for d in (3, 2, 1, 0)], 1)
    q = r % 8
    kk = np.arange(120)[None, :]
    off = kk - 56
    inside = (off >= 0) & (off < 8)
    c["new_diff"] = np.where(inside & (off <= q), 0, NEG).astype(f)
    c["new_win"] = np.where(inside, log_count(np.where(inside, q - off, 0)), NEG).astype(f)
    j = np.arange(NWIN)
    pos = np.where(j < 768, 16 * (j // 8) + j % 8, 1536 + j - 768)
    c["old_win"] = log_count(PAST + q - pos[None, :])
    pair = np.zeros((P, 32), f)
    for h in range(HA):
        for s in range(2):
            for i in range(8):
                pair[32 * h + 8 * s + i, 8 * h + i] = 1
    c["pair"] = pair
    inv = (f(500000.0) ** (-np.arange(8, dtype=f) / f(8))).astype(f)
    rope = np.zeros((P, NT, 2, 8), f)
    for t in range(NT):
        p = (t * P + np.arange(P)) if t < 4 else PAST + np.arange(P) % 8
        ang = (p.astype(f)[:, None] * inv[None, :]).astype(f)
        rope[:, t, 0], rope[:, t, 1] = np.cos(ang), np.sin(ang)
    c["rope"] = rope.reshape(P, -1)
    sub = (np.arange(P) % 32) // 8
    c["coef_one"] = (sub != 1).astype(f)[:, None]
    c["coef_lam"] = -(sub == 1).astype(f)[:, None]
    e = np.arange(NE, dtype=f)
    c["expert_rank"] = np.broadcast_to(NE - e, (P, NE)).astype(f)
    c["expert_base"] = np.broadcast_to(P * e, (P, NE)).astype(f)
    c["expert_shift"] = np.broadcast_to(P * (31 - e), (P, NE)).astype(f)
    c["group_rank"] = np.broadcast_to(4 - np.arange(4, dtype=f), (P, 4)).astype(f)
    code = np.zeros((P, 2, NT, 2), f)
    for t in range(NT):
        for s in range(2):
            code[:, s, t, 0] = t * P + np.arange(P)
            code[:, s, t, 1] = 2 * (t * P + np.arange(P)) + s
    c["codes"] = code.reshape(P, -1)
    valid = np.ones((P, NT), f)
    valid[TS:, 4] = 0
    c["valid"] = valid
    c["extra_no"] = np.broadcast_to(np.arange(NX, dtype=f), (P, NX)).astype(f)
    return c


PARAMS = [("gain", 32), ("subln", 1), ("w_dw", KC * CK), ("b_dw", KC), ("ln_g", KC), ("ln_b", KC),
          ("b_pw1", 16), ("router", 2 * KC * 36), ("lambdas", 4)]


def build(nc, x_prompt, x_sample, ck, cv, wk, wv, st_rows, st_cols, ptab, w_in, w_out, w_pw1, w_pw2,
          w_g, w_u, w_d, params, consts, vecs,
          y_p, y_s, nkd_p, nvd_p, nkd_s, nvd_s, nwk_p, nwv_p, nwk_s, nwv_s, ncv_p, ncv_s):
    f32, i32 = mybir.dt.float32, mybir.dt.int32
    ALU, ACT, AX = mybir.AluOpType, mybir.ActivationFunctionType, mybir.AxisListType
    ctx = ExitStack()

    def sb(name, shape, dt=f32):
        return ctx.enter_context(nc.sbuf_tensor(name, shape, dt))

    def sem(name):
        return ctx.enter_context(nc.semaphore(name))

    def scratch(name, shape):
        return nc.dram_tensor(name, shape, f32).ap()

    h_rows = [scratch(f"h_rows{l}", (T, D)) for l in range(2)]
    y_rows = [scratch(f"y_rows{l}", (2 * T, D)) for l in range(2)]
    table = [scratch(f"table{l}", ((NE + NX) * P, 2)) for l in range(2)]

    ring = sb("ring", [P, 6, 4096])
    x = sb("x", [P, NT * D])
    act_t = sb("act_t", [P, KC, T])
    big = sb("big", [P, 14848])
    cst_np = constants()
    ccol, o = {}, 0
    for name, a in cst_np.items():
        ccol[name] = (o, a.shape[1])
        o += a.shape[1]
    cst = sb("cst", [P, o])
    pcol, o = {}, 0
    for name, w in PARAMS:
        pcol[name] = (o, w)
        o += w
    par = sb("par", [P, o])
    st = sb("st", [P, 112])
    sti = sb("sti", [P, 112], i32)
    pt_sb = sb("pt_sb", [1, NB * NPG], i32)

    def C(name):
        a, w = ccol[name]
        return cst[:, a:a + w]

    def PR(name):
        a, w = pcol[name]
        return par[:, a:a + w]

    xt = x[:, :].rearrange("p (t d) -> p t d", t=NT)
    ident, ones = C("ident"), C("ones")
    gain = PR("gain").rearrange("p (u k) -> p u k", u=4)
    router = PR("router").rearrange("p (l k e) -> p l k e", l=2, k=KC)
    rope = C("rope").rearrange("p (t s d) -> p t s d", t=NT, s=2)
    codes = C("codes").rearrange("p (s t c) -> p s t c", s=2, t=NT)

    def B(a, n, *shape):
        v = big[:, a:a + n]
        if len(shape) == 2:
            v = v.rearrange("p (a b) -> p a b", a=shape[0])
        elif len(shape) == 3:
            v = v.rearrange("p (a b c) -> p a b c", a=shape[0], b=shape[1])
        return v

    def X(a, n, *shape):
        v = x[:, a:a + n]
        if len(shape) == 2:
            v = v.rearrange("p (a b) -> p a b", a=shape[0])
        elif len(shape) == 3:
            v = v.rearrange("p (a b c) -> p a b c", a=shape[0], b=shape[1])
        return v

    qT = [B(0, 2048, 4, 512), B(6144, 2048, 4, 512)]
    kT = [B(2048, 2048, 4, 512), B(8192, 2048, 4, 512)]
    vP = [B(4096, 2048, 4, 512), B(10240, 2048, 4, 512)]
    qS = [B(12288, 576, 9, 4, 16), B(12800, 576, 9, 4, 16)]
    kS = [B(13312, 256, 4, 64), B(13568, 256, 4, 64)]
    vS = [B(13824, 512), B(14336, 512)]
    zrow = X(0, 2048, 4, 512)
    PTsb = X(0, 2048, 2, 2, 512)
    Ex = X(2048, 2048, 2, 2, 512)
    orow = X(4096, 256, 2, 128)
    rtmp = X(4352, 256, 4, 8, 8)
    S_d, S_w = B(0, 2112), B(2112, 1344)
    KTs = B(3456, 4096, 8, 512)
    PT_d, PT_w = B(7552, 2176, 17, 128), B(9728, 1408, 11, 128)
    aux = X(0, 2048, 4, 512)
    O_all = [X(2048, 1024, 8, 128), X(3072, 1024, 8, 128)]
    Qcur = X(4096, 256, 2, 4, 32)
    comb, csq = B(0, 1024, 8, 128), B(1024, 1024, 8, 128)
    xn = B(11776, 2048, 2, D)
    Xg, XgT = B(0, 2048, 2, D), B(2048, 2048, 2, KC, P)
    sg, hb, hbT = B(4096, 512), B(4608, 512), B(5120, 512, 4, P)
    Y = B(5632, 2048, 2, D)
    y01 = B(7680, 4096, 2, 2, D)
    u_ext = B(0, KC * UE, KC, UE)
    cc = B(KC * UE, KC * T, KC, T)
    sig = B(11376, 2 * T, 2, T)
    mr = B(12528, 2 * T, 2, T)
    brow = big[0:1, 13680:13680 + D]
    crow_p, crow_s = B(12528, D)[0:CK - 1], B(12528 + D, D)[0:TS]
    osq = X(4608, 128)
    gf = B(0, D)

    ps = ctx.enter_context(nc.psum_tensor("ps", [P, 8, 512], f32))

    waited = sem("waited")
    stage = {n: sem(f"stage_{n}") for n in ("pe", "act", "dve", "pool")}
    act_step, dve_step, pool_step = sem("act_step"), sem("dve_step"), sem("pool_step")
    loaded = [sem(f"loaded{s}") for s in range(6)]
    consts_in, table_io = sem("consts_in"), sem("table_io")
    rows_out2 = [sem(f"rows_out_{i}") for i in range(2)]
    out_done, copy_done = sem("out_done"), sem("copy_done")
    norm_sq, norm_rows, norm_tr, norm_ev = sem("norm_sq"), sem("norm_rows"), sem("norm_tr"), sem("norm_ev")
    z_mm, z_copy, z_rope, z_tr, z_tev = sem("z_mm"), sem("z_copy"), sem("z_rope"), sem("z_tr"), sem("z_tev")
    z_out = [sem(f"z_out{i}") for i in range(4)]
    a_s, a_max, a_exp, a_p, a_t, a_ptev = sem("a_s"), sem("a_max"), sem("a_exp"), sem("a_p"), sem("a_t"), sem("a_ptev")
    r_slot = sem("r_slot")
    a_o, a_sq, a_row, a_ot, a_cat = sem("a_o"), sem("a_sq"), sem("a_row"), sem("a_ot"), sem("a_cat")
    q_ready, t_done, te_act, te_dve, s_mm = sem("q_ready"), sem("t_done"), sem("te_act"), sem("te_dve"), sem("s_mm")
    sd_ev, sw_ev, max_ready, exp_done = sem("sd_ev"), sem("sw_ev"), sem("max_ready"), sem("exp_done")
    pt_done, ptev_act, ptev_dve, pv_done, o_ev = sem("pt_done"), sem("ptev_act"), sem("ptev_dve"), sem("pv_done"), sem("o_ev")
    aux_in = [sem("auxk_in"), sem("auxv_in")]
    f_mm, f_ev, x_in = sem("f_mm"), sem("f_ev"), sem("x_in")
    p_mm, p_ev = sem("p_mm"), sem("p_ev")
    r_mm, r_ev, r_exp = sem("r_mm"), sem("r_ev"), sem("r_exp")
    lam_mm, lam_exp, lam_ready, zeroed = sem("lam_mm"), sem("lam_exp"), sem("lam_ready"), sem("zeroed")
    moe = []
    for l in range(2):
        for kind in ("m", "x"):
            m = {n: sem(f"{kind}{l}_{n}") for n in (
                "gathered0", "gathered1", "xt", "xgt", "g", "silu", "u", "hb", "ht", "hbt", "y", "yev",
                "scattered0", "scattered1")}
            moe.append(m)
    x_loaded = [sem(f"x_loaded{l}") for l in range(2)]
    y_back = [sem("y_back0"), sem("y_back1")]
    y_used, tok_ready, code_ready = sem("y_used"), sem("tok_ready"), sem("code_ready")
    x_ready = [sem("x_ready0"), sem("x_ready1")]
    pw_mm, pw_sig, glu, state_in = sem("pw_mm"), sem("pw_sig"), sem("glu"), sem("state_in")
    cv_new, var_ready, root = sem("cv_new"), sem("var_ready"), sem("root")
    cv_tr, cv_ev, mean_mm, centred, squared, var_mm, normed, silu_c = (
        sem("cv_tr"), sem("cv_ev"), sem("mean_mm"), sem("centred"), sem("squared"), sem("var_mm"),
        sem("normed"), sem("silu_c"))

    class Steps:
        def __init__(self, eng, s):
            self.eng, self.s, self.base, self.k = eng, s, 0, 0

        @property
        def n(self):
            return self.base + self.k

        def start(self, base):
            self.base, self.k = base, 0

        def __call__(self, ins):
            ins.then_inc(self.s, 1)
            self.k += 1
            return ins

        def done(self):
            self.eng.wait_ge(self.s, self.n)


    NAMES = ("pe", "act", "dve", "pool")

    class Fence:
        def __init__(self, eng, name):
            self.eng, self.name, self.n = eng, name, 0

        def __call__(self):
            self.n += 1
            self.eng.drain().then_inc(stage[self.name], 1)
            for o in NAMES:
                self.eng.wait_ge(stage[o], self.n)

    with_lead = [s_mm, pv_done, te_act, te_dve, sw_ev, o_ev, ptev_act, ptev_dve]
    with_lead += [m[n] for m in moe for n in ("xgt", "g", "silu", "u", "hb", "ht", "hbt", "y", "yev")]

    PER_BATCH = [128, 128, 128, 128, 112, 112]
    AFTER_BATCH = [16 + NB * n for n in PER_BATCH]

    def slot(s, a):
        return ring[:, s, :].rearrange("p (a n) -> p a n", a=a)

    def eslots(par):
        return (2, 3, 4) if par == 0 else (5, 0, 1)

    def moe_base(l, s):
        return AFTER_BATCH[s] + (16 if s < 2 else 0) + l * (16 * 16 + 16)

    qtab = {0: 0, 1: 1, 3: 2, 4: 3}

    def stores_before(k):
        return sum(1 for i in range(k % 4, k, 4) if i // NT in (1, 3) and i < 4 * NT)

    GROUPS = [None, (0, 0, 4, 0), (0, 4, 4, 512), (1, 0, 4, 1024), (1, 4, 4, 1536),
              (4, 0, 4, 0), (4, 4, 4, 512), (None, 0, 2, 1024)]
    CHUNKS = [(0, range(0, 4)), (0, range(4, 8)), (0, range(8, 12)), (0, range(12, 16)), (0, range(16, 17)),
              (1, range(0, 4)), (1, range(4, 8)), (1, range(8, 11))]
    ITEMS = [(qt, kind, c) for qt in range(4) for c in range(4) for kind in (0, 1)]
    NI = len(ITEMS)


    rcol = {"n": 0}

    def R(*shape):
        n = int(np.prod(shape))
        a = rcol["n"]
        rcol["n"] += n
        return B(a, n, *shape) if len(shape) > 1 else B(a, n)

    L = R(NT, 36)
    g_max, g_sub, g_exp, g_hit, g_top = R(NT), R(NT, 4), R(NT, 4), R(NT, 4), R(NT)
    g_one, g_pen, g_sum, e_all = R(NT, 4), R(NT, 4), R(NT), R(NT, NE)
    m_1, m_2, top, hit = R(NT), R(NT), R(NT), R(NT, NE)
    one = [R(NT, NE), R(NT, NE)]
    e_dif, e_exp, both = R(NT), R(NT), R(NT, NE)
    rank, slot_f, pick = R(NT, NE), R(NT, NE), R(NT, NE)
    count, more, pre_a, pre_b, shift_f = R(NE), R(NE), R(NE), R(NE), R(NE)
    slots, x_hit, x_exp = R(2, NT), R(NX, NE), R(NX)
    tab = B(2560, 256, P, 2)[0:NE + NX]
    wts = st[:, 100:110].rearrange("p (s t) -> p s t", s=2)
    tokI, codeI = sti[:, 0:40], sti[:, 40:80]
    tokS, codeS, slotI = sti[:, 80:82], sti[:, 82:84], sti[:, 100:110]

    def shift(eng, b):
        n = PAST - NQ
        for dst, src in ((nwk_s, wk), (nwv_s, wv)):
            eng.dma_start(dst[b, 0:n].rearrange("a c -> (a c)").rearrange("(k n) -> k n", k=16),
                          src[b, NQ:PAST].rearrange("a c -> (a c)").rearrange("(k n) -> k n", k=16)
                          ).then_inc(copy_done, 16)

    block = ctx.enter_context(nc.Block())

    @block.sync
    def _(sp):
        sp.dma_start(cst[:, :], consts).then_inc(consts_in, 16)
        sp.dma_start(par[:, :], params).then_inc(consts_in, 16)
        sp.dma_start(pt_sb[:, :], ptab).then_inc(consts_in, 16)
        wi = w_in.rearrange("(k p) (n c) -> n p k c", p=P, n=6)
        for n in range(6):
            sp.dma_start(slot(n, 8), wi[n]).then_inc(loaded[n], 16)
        sp.wait_ge(consts_in, 48)

        def request(b, s_free):
            pages = [sp.value_load(pt_sb[0:1, bass.ds(b * NPG + i, 1)], min_val=0, max_val=ck.shape[0] - 1)
                     for i in range(NPG)]
            for half in range(2):
                s_free(half)
                for i in range(8):
                    sp.dma_start(slot(half, 8)[:, i, :],
                                 ck[bass.ds(pages[8 * half + i], 1)].rearrange("a p c -> (a p) c")
                                 ).then_inc(loaded[half], 16)
            for src, s, a in ((wk, 4, 0), (wv, 5, 1)):
                if a == 0:
                    s_free(4)
                    s_free(6)
                else:
                    for half in range(2):
                        s_free(2 + half)
                        for i in range(8):
                            sp.dma_start(slot(2 + half, 8)[:, i, :],
                                         cv[bass.ds(pages[8 * half + i], 1)].rearrange("a p c -> (a p) c")
                                         ).then_inc(loaded[2 + half], 16)
                    s_free(5)
                    s_free(7)
                one = src[bass.ds(b, 1)].rearrange("a r c -> (a r) c")
                far = one[0:1536].rearrange("(t g r) c -> t g r c", t=6, r=16)[:, :, 0:8]
                for i in range(6):
                    sp.dma_start(slot(s, 8)[:, i, :], far[i]).then_inc(loaded[s], 16)
                recent = one[1536:2048].rearrange("(t p) c -> p t c", p=P)
                sp.dma_start(slot(s, 8)[:, 6:8, :], recent[:, 0:2]).then_inc(loaded[s], 16)
                sp.dma_start(aux[:, 2 * a:2 * a + 2, :], recent[:, 2:4]).then_inc(aux_in[a], 16)

        def first_free(i):
            if i < 6:
                sp.wait_ge(z_mm, 5 * (i + 1))
            else:
                sp.wait_ge(stage["dve"], 3)
                sp.wait_ge(stage["pe"], 3)
                sp.wait_ge(stage["act"], 3)
                sp.wait_ge(stage["pool"], 3)
        request(0, first_free)
        with sp.Fori(1, NB) as b:
            def later_free(i):
                if i in (0, 1, 4, 6):
                    sp.wait_ge(t_done, (b - 1) * 28 + {0: 8, 1: 16, 4: 24, 6: 28}[i])
                    sp.sem_inc(waited)
                else:
                    sp.wait_ge(pv_done, (b - 1) * 8 + {2: 2, 3: 4, 5: 7, 7: 8}[i] + 1)
                    sp.sem_inc(waited)
            request(b, later_free)

        wo = w_out.rearrange("(k p) (n c) -> n p k c", p=P, n=2)
        for n in range(2):
            sp.wait_ge(t_done, (NB - 1) * 28 + 8 * (n + 1))
            sp.dma_start(slot(n, 8), wo[n]).then_inc(loaded[n], 16)

        def expert_load(l, e, par, kind, free):
            s = eslots(par)[kind]
            free(kind)
            src = (w_g, w_u, w_d)[kind][bass.ds(e + NE * l, 1)].rearrange("a r c -> (a r) c")
            src = src.rearrange("(k p) c -> p k c", p=P)
            sp.dma_start(slot(s, 8 if kind < 2 else 4), src).then_inc(loaded[s], 16)

        def moe_weights(l):
            m, mx = moe[2 * l], moe[2 * l + 1]

            def earlier(par):
                def free(kind):
                    s = eslots(par)[kind]
                    if l == 0:
                        if s < 2:
                            sp.wait_ge(p_mm, NT * (s + 1))
                        elif s in (2, 3):
                            sp.wait_ge(pv_done, (NB - 1) * 8 + (2, 4)[s - 2] + 1)
                        elif s == 4:
                            sp.wait_ge(t_done, (NB - 1) * 28 + 24)
                        else:
                            sp.wait_ge(pv_done, (NB - 1) * 8 + 8)
                    else:
                        if s < 2:
                            sp.wait_ge(p_mm, 2 * NT + NT * (s + 1))
                        else:
                            sp.wait_ge(pw_mm, 4 if s < 4 else 8)
                return free

            for kind in range(3):
                expert_load(l, 0, 0, kind, earlier(0))
            for kind in range(3):
                expert_load(l, 1, 1, kind, earlier(1))
            with sp.Fori(1, NE // 2) as j:
                for par_ in range(2):
                    def free(kind, par_=par_):
                        n = 2 * j - 1 + par_
                        if kind < 2:
                            sp.wait_ge(m["gu"[kind]], n + 1)
                            sp.sem_inc(waited)
                        else:
                            sp.wait_ge(m["y"], 2 * n + 1)
                            sp.sem_inc(waited)
                    for kind in range(3):
                        expert_load(l, 2 * j + par_, par_, kind, free)
            sp.wait_ge(m["y"], 2 * NE + 1)
            n_extra = sp.value_load(sti[0:1, 96:97], min_val=0, max_val=NX)
            with sp.Fori(0, NX) as j:
                with sp.If(n_extra > j):
                    e = sp.value_load(sti[0:1, bass.ds(j + 88, 1)], min_val=0, max_val=NE - 1)
                    sp.wait_ge(mx["y"], 2 * j + 1)
                    sp.sem_inc(waited)
                    for kind in range(3):
                        src = (w_g, w_u, w_d)[kind][bass.ds(e + NE * l, 1)].rearrange("a r c -> (a r) c")
                        src = src.rearrange("(k p) c -> p k c", p=P)
                        sp.dma_start(slot(2 + kind, 8 if kind < 2 else 4), src).then_inc(x_loaded[l], 16)
                    sp.wait_ge(mx["y"], 2 * j + 3)
                    sp.sem_inc(waited)

        moe_weights(0)
        w1 = w_pw1.rearrange("(k p) (n c) -> n p k c", p=P, n=4)
        for s, n in ((2, 0), (3, 2), (4, 1), (5, 3)):
            sp.dma_start(slot(s, 8), w1[n]).then_inc(loaded[s], 16)
        w2 = w_pw2.rearrange("(k p) (n c) -> n p k c", p=P, n=2)
        for n in range(2):
            sp.dma_start(slot(n, 8), w2[n]).then_inc(loaded[n], 16)
        for b in range(NB // 2, NB):
            shift(sp, b)
        moe_weights(1)
        sp.wait_ge(copy_done, 2 * NB * 16 + 16)

    @block.scalar
    def _(act):
        A = Steps(act, act_step)
        fence = Fence(act, "act")
        A_ = nc.scalar.activation
        for b in range(NB // 2):
            shift(act, b)
        act.dma_start(ncv_s[:, 0:CK - 1 - NQ, :], st_rows[:, NQ:, :]).then_inc(copy_done, 16)

        def copy(o, i):
            return A_(o, i, ACT.Copy)

        def norm(u):
            for t in range(NT):
                r = rows(t)
                if t:
                    A.done()
                A(A_(xn[0:r, 0, :], xt[0:r, t, :], ACT.Square, accum_out=st[0:r, t:t + 1]))
            A.done()
            act.drain().then_inc(norm_sq, 1)

        act.wait_ge(lam_mm, 1)
        A_(st[:, 20:22], ps[:, 7, 0:2], ACT.Exp).then_inc(lam_exp, 1)
        act.wait_ge(x_in, 32)
        act.wait_ge(zeroed, 1)
        norm(0)
        fence()

        i_z = 0
        for n in range(6):
            for t in range(NT):
                r = rows(t)
                act.wait_ge(z_mm, i_z + 1)
                bank = ps[0:r, 4 + i_z % 4, :]
                i_z += 1
                if n in qtab:
                    k = qtab[n] * NT + t
                    if k > 3:
                        act.wait_ge(z_tr, k - 3)
                    if 16 * stores_before(k) > 0:
                        act.wait_ge(z_out[k % 4], 16 * stores_before(k))
                    if n < 2:
                        copy(zrow[0:r, k % 4, :].rearrange("p (h s d) -> p s h d", h=4, s=2),
                             bank.rearrange("p (s h d) -> p s h d", h=4, s=2)).then_inc(z_copy, 1)
                    else:
                        copy(zrow[0:r, k % 4, :], bank).then_inc(z_copy, 1)
                else:
                    dst = vP[n // 4][:, t, :] if t < 4 else vS[n // 4][0:r, :]
                    copy(dst, bank).then_inc(z_copy, 1)
        fence()

        for s in range(NI + 3):
            if s < NI:
                qt, kind, c = ITEMS[s]
                n = (qt + 1) * P
                act.wait_ge(a_max, s + 1)
                if s > 1:
                    act.wait_ge(a_t, s - 1)
                if s > 1:
                    act.wait_ge(a_p, s - 1)
                for j in range(2):
                    a = 2 * (s % 2) + j
                    A_(Ex[:, s % 2, j, 0:n], ps[:, a, 0:n], ACT.Exp, bias=st[:, 32 + a:33 + a],
                       scale=(SCALE if kind == 0 else 1.0), accum_out=st[:, 36 + a:37 + a]).then_inc(a_exp, 1)
            m = s - 1
            if 0 <= m < NI:
                qt, kind, c = ITEMS[m]
                n = (qt + 1) * P
                act.wait_ge(a_t, m + 1)
                if m > 1:
                    act.wait_ge(a_o, m - 1)
                if kind == 0:
                    copy(PTsb[:, m % 2, 0, 0:n], ps[:, 4, 0:n]).then_inc(a_ptev, 1)
                else:
                    copy(PTsb[:, m % 2, :, 0:n], ps[:, 4:6, 0:n]).then_inc(a_ptev, 1)
            m = s - 2
            if 0 <= m < NI and ITEMS[m][1] == 0:
                act.wait_ge(a_o, m + 1)
                if m > 0:
                    act.wait_ge(a_row, m)
                if A.k:
                    A.done()
                A(A_(osq, ps[:, 6, 0:P], ACT.Square, accum_out=st[:, 44:45]))
                A.done()
                act.drain().then_inc(a_sq, 1)
        fence()
        fence()

        with act.Fori(0, NB) as b:
            def tev(g):
                nb = GROUPS[g][2]
                for c in (0, 2):
                    act.wait_ge(t_done, b * 28 + 4 * (g - 1) + c + 1)
                    act.wait_ge(s_mm, (b * 8 + (0 if g <= 2 else g - 1)) + 1)
                    copy(KTs[:, 4 * (g % 2) + c, 0:nb * P], ps[:, 0, 0:nb * P]).then_inc(te_act, 1)

            def sd(g):
                act.wait_ge(s_mm, b * 8 + g + 2)
                act.wait_ge(pv_done, b * 8 + 1)
                copy(S_d[:, (g - 1) * 512:g * 512], ps[:, 2 + g % 2, :]).then_inc(sd_ev, 1)

            tev(1); tev(2); sd(1); tev(3); sd(2); tev(4); sd(3); tev(5); sd(4); tev(6)
            act.wait_ge(max_ready, b * 2 + 1)
            A_(S_d, S_d, ACT.Exp, bias=st[:, 48:49], scale=SCALE, accum_out=st[:, 50:51]).then_inc(exp_done, 1)
            tev(7)
            act.wait_ge(max_ready, b * 2 + 2)
            A_(S_w, S_w, ACT.Exp, bias=st[:, 49:50], scale=1.0, accum_out=st[:, 51:52]).then_inc(exp_done, 1)
            for k in (1, 3, 5):
                w, blocks = CHUNKS[k]
                act.wait_ge(pt_done, b * 8 + k + 1)
                copy((PT_w if w else PT_d)[:, blocks[0]:blocks[-1] + 1, :],
                     ps[:, 5, :].rearrange("p (n c) -> p n c", c=P)).then_inc(ptev_act, 1)
            act.wait_ge(pt_done, b * 8 + 8)
            copy(PT_w[:, 8:10, :], ps[:, 5, 0:256].rearrange("p (n c) -> p n c", c=P)).then_inc(ptev_act, 1)
            copy(PT_w[0:TS, 10, :], ps[0:TS, 5, 256:384]).then_inc(ptev_act, 1)
        fence()
        act.wait_ge(f_mm, 1)
        copy(comb[0:32, :, :].rearrange("p b d -> p (b d)"),
             ps[0:32, 0:2, :].rearrange("p a n -> p (a n)")).then_inc(f_ev, 1)
        fence()
        fence()

        def silu_step(m, n):
            act.wait_ge(m["g"], n + 2)
            act.wait_ge(m["hb"], n + 1)
            A_(sg, ps[:, 0, :], ACT.Silu).then_inc(m["silu"], 1)

        def hbt_step(m, n):
            act.wait_ge(m["ht"], n + 2)
            act.wait_ge(m["y"], 2 * n + 1)
            copy(hbT, ps[:, 4, :].rearrange("p (k c) -> p k c", k=4)).then_inc(m["hbt"], 1)

        def y_step(m, n, par_, used):
            for h in range(2):
                act.wait_ge(m["y"], 2 * n + h + 2)
                if used is not None and h == 0:
                    act.wait_ge(m[f"scattered{par_}"], used)
                copy(Y[:, par_, h * 512:(h + 1) * 512], ps[:, 5 + h, :]).then_inc(m["yev"], 1)

        def layer_ffn(l):
            norm(1 + 2 * l)
            fence()
            act.wait_ge(r_ev, 3 * l + 1)
            A_(g_exp, g_sub, ACT.Exp).then_inc(r_exp, 1)
            act.wait_ge(r_ev, 3 * l + 2)
            A_(e_exp, e_dif, ACT.Exp).then_inc(r_exp, 1)
            fence()
            m, mx = moe[2 * l], moe[2 * l + 1]
            silu_step(m, 0)
            silu_step(m, 1); hbt_step(m, 0); y_step(m, 0, 0, None)
            silu_step(m, 2); hbt_step(m, 1); y_step(m, 1, 1, None)
            with act.Fori(1, NE // 2 - 1) as j:
                silu_step(m, 2 * j + 1); hbt_step(m, 2 * j); y_step(m, 2 * j, 0, j * 16)
                silu_step(m, 2 * j + 2); hbt_step(m, 2 * j + 1); y_step(m, 2 * j + 1, 1, j * 16)
            silu_step(m, NE - 1); hbt_step(m, NE - 2); y_step(m, NE - 2, 0, 15 * 16)
            hbt_step(m, NE - 1); y_step(m, NE - 1, 1, 15 * 16)
            n_extra = act.value_load(sti[0:1, 96:97], min_val=0, max_val=NX)
            act.wait_ge(m["scattered0"], 16 * 16)
            with act.Fori(0, NX) as j:
                with act.If(n_extra > j):
                    silu_step(mx, j); hbt_step(mx, j); y_step(mx, j, 0, None)
            fence()

        layer_ffn(0)
        norm(2)
        fence()
        for ch in range(KC):
            act.wait_ge(pw_mm, ch + 1)
            if ch > 1:
                act.wait_ge(glu, ch - 1)
            bank = 4 * (ch % 2)
            A_(sig[:, ch % 2, :].rearrange("p (h n) -> p h n", h=2), ps[:, bank + 2:bank + 4, 0:HALF],
               ACT.Sigmoid, bias=PR("b_pw1")[:, 8 + ch:9 + ch], scale=1.0).then_inc(pw_sig, 1)
        act.wait_ge(glu, KC)
        copy(act_t[:, :, 0:TS].rearrange("p c (b q) -> p c b q", b=NB),
             u_ext[:, :, CK - 1 + TP:].rearrange("p c (b w) -> p c b w", b=NB)[:, :, :, CK - 1:]).then_inc(cv_new, 1)
        act.wait_ge(cv_tr, 1)
        copy(crow_p, ps[0:CK - 1, 0:2, :].rearrange("p a n -> p (a n)")).then_inc(cv_ev, 1)
        copy(crow_s, ps[0:TS, 2:4, :].rearrange("p a n -> p (a n)")).then_inc(cv_ev, 1)
        fence()
        act.wait_ge(centred, 1)
        for ch in range(KC):
            if ch > 1:
                act.wait_ge(var_mm, ch - 1)
            A_(sig[:, ch % 2, :], cc[:, ch, :], ACT.Square).then_inc(squared, 1)
        act.wait_ge(var_ready, 1)
        A_(mr[:, 1, :], mr[:, 1, :], ACT.Sqrt).then_inc(root, 1)
        for ch in range(KC):
            act.wait_ge(normed, ch + 1)
            A_(cc[:, ch, :], cc[:, ch, :], ACT.Silu, bias=PR("ln_b")[:, ch:ch + 1],
               scale=PR("ln_g")[:, ch:ch + 1]).then_inc(silu_c, 1)
        fence()
        fence()
        layer_ffn(1)
        norm(4)

    @block.vector
    def _(dve):
        V = nc.vector
        S = Steps(dve, dve_step)
        fence = Fence(dve, "dve")

        def link(ins):
            S(ins)
            S.done()

        V.memset(st[:, :], 1.0).then_inc(zeroed, 1)
        dve.wait_ge(zeroed, 1)
        dve.wait_ge(consts_in, 48)
        lam4 = PR("lambdas")
        link(V.tensor_tensor(st[:, 22:23], lam4[:, 0:1], lam4[:, 1:2], ALU.mult))
        S(V.tensor_tensor(st[:, 23:24], lam4[:, 2:3], lam4[:, 3:4], ALU.mult))
        S.done()
        dve.drain().then_inc(lam_ready, 1)
        dve.wait_ge(lam_exp, 1)
        link(V.tensor_tensor(st[:, 25:26], st[:, 20:21], st[:, 21:22], ALU.subtract))
        link(V.tensor_scalar(st[:, 25:26], st[:, 25:26], LAM_INIT, None, ALU.add))
        link(V.scalar_tensor_tensor(st[:, 24:25], C("coef_lam"), st[:, 25:26], C("coef_one"), ALU.mult, ALU.add))
        link(V.tensor_scalar(st[:, 25:26], st[:, 25:26], -1.0, None, ALU.mult))

        def rstd(o, i, n):
            p, w = o.shape
            v, half, t = (st[0:p, a:a + w] for a in (70, 78, 86))
            link(V.tensor_scalar(v, i, 1.0 / n, EPS, ALU.mult, ALU.add))
            link(V.tensor_scalar(half, v, -0.5, None, ALU.mult))
            link(V.tensor_scalar(t.bitcast(i32), v.bitcast(i32), 1, None, ALU.arith_shift_right))
            link(V.tensor_scalar(o.bitcast(i32), t.bitcast(i32), -1, 0x5f3759df, ALU.mult, ALU.add))
            for _ in range(3):
                link(V.tensor_tensor(t, o, o, ALU.mult))
                link(V.tensor_tensor(t, t, half, ALU.mult))
                link(V.scalar_tensor_tensor(o, t, 1.5, o, ALU.add, ALU.mult))

        def norm(u):
            dve.wait_ge(norm_sq, u + 1)
            rstd(st[:, 5:10], st[:, 0:5], D)

            def turned(t):
                r = rows(t)
                dve.wait_ge(norm_tr, NT * u + t + 1)
                src = ps[:, 2 * (t % 2):2 * (t % 2) + 2, :].rearrange("p a (k c) -> p (a k) c", k=4)
                V.tensor_tensor(act_t[:, :, t * P:t * P + r], src[:, :, 0:r],
                                gain[:, u, :].unsqueeze(2).broadcast_to((P, KC, r)), ALU.mult).then_inc(norm_ev, 1)

            for t in range(NT):
                r = rows(t)
                if t >= 2:
                    dve.wait_ge(norm_tr, NT * u + t - 1)
                    if u in (1, 3):
                        dve.wait_ge(rows_out2[t % 2], 16 * ((u // 2) * (3 - t % 2) + t // 2))
                V.tensor_scalar(xn[0:r, t % 2, :], xt[0:r, t, :], st[0:r, 5 + t:6 + t], None,
                                ALU.mult).then_inc(norm_rows, 1)
                if t:
                    turned(t - 1)
            turned(NT - 1)

        norm(0)
        fence()

        def z_turned(n, t, k):
            dve.wait_ge(z_tr, k + 1)
            src = ps[:, k % 2, :].rearrange("p (h c) -> p h c", h=4)
            w = n // 3
            if t < 4:
                dst = (kT if n in (1, 4) else qT)[w]
                V.tensor_copy(dst[:, :, t * P:(t + 1) * P], src).then_inc(z_tev, 1)
            elif n in (1, 4):
                V.tensor_copy(kS[w], src[:, :, 0:TS]).then_inc(z_tev, 1)
            else:
                for j in range(2):
                    p = slice(64 * j, 64 * j + 64)
                    for h in range(4):
                        ins = V.tensor_copy(qS[w][p, 0:NB, h, 8 * j:8 * j + 8],
                                            src[p, h, 0:TS].rearrange("p (b q) -> p b q", b=NB))
                        if j == 1 and h == 3:
                            ins.then_inc(z_tev, 1)

        link(V.memset(B(12288, 1024), 0.0))
        prev = None
        i_z = 0
        for n in range(6):
            for t in range(NT):
                i_z += 1
                if n not in qtab:
                    continue
                r, k = rows(t), qtab[n] * NT + t
                dve.wait_ge(z_copy, i_z)
                if k > 0:
                    dve.wait_ge(z_rope, k)
                z3 = zrow[0:r, k % 4, :].rearrange("p (g d) -> p g d", g=8)
                x1, x2 = z3[:, :, 0:8], z3[:, :, 8:16]
                cos = rope[0:r, t, 0:1, :].broadcast_to((r, 8, 8))
                sin = rope[0:r, t, 1:2, :].broadcast_to((r, 8, 8))
                S(V.tensor_tensor(rtmp[0:r, 0], x1, cos, ALU.mult))
                S(V.tensor_tensor(rtmp[0:r, 1], x2, sin, ALU.mult))
                S(V.tensor_tensor(rtmp[0:r, 2], x2, cos, ALU.mult))
                S(V.tensor_tensor(rtmp[0:r, 3], x1, sin, ALU.mult))
                S.done()
                S(V.tensor_tensor(x1, rtmp[0:r, 0], rtmp[0:r, 1], ALU.subtract))
                V.tensor_tensor(x2, rtmp[0:r, 2], rtmp[0:r, 3], ALU.add).then_inc(z_rope, 1)
                if prev:
                    z_turned(*prev)
                prev = (n, t, k)
        z_turned(*prev)
        fence()

        for s in range(NI + 3):
            if s < NI:
                qt, kind, c = ITEMS[s]
                n = (qt + 1) * P
                a = 2 * (s % 2)
                dve.wait_ge(a_s, s + 1)
                if 2 * (s - 1) > 0:
                    dve.wait_ge(a_exp, 2 * (s - 1))
                sc = ps[:, a:a + 2, 0:n]
                if kind == 0:
                    diag = ps[:, a:a + 2, n - P:n]
                    link(V.tensor_tensor(diag, diag, C("causal").unsqueeze(1).broadcast_to((P, 2, P)), ALU.add))
                else:
                    msk = C("dilated")[:, (3 - qt) * P:].unsqueeze(1).broadcast_to((P, 2, n))
                    link(V.scalar_tensor_tensor(sc, sc, SCALE, msk, ALU.mult, ALU.add))
                link(V.tensor_reduce(st[:, 32 + a:34 + a], sc, AX.X, ALU.max))
                V.tensor_scalar(st[:, 32 + a:34 + a], st[:, 32 + a:34 + a], -SCALE if kind == 0 else -1.0, None,
                                ALU.mult).then_inc(a_max, 1)
            m = s - 2
            if 0 <= m < NI:
                a = 2 * (m % 2)
                dve.wait_ge(a_o, m + 1)
                if m > 1:
                    dve.wait_ge(a_ot, m - 1)
                if ITEMS[m][1] == 0:
                    dve.wait_ge(a_sq, sum(1 for i in range(m + 1) if ITEMS[i][1] == 0))
                    rstd(st[:, 45:46], st[:, 44:45], P)
                    V.tensor_scalar(orow[:, m % 2, :], ps[:, 6, 0:P], st[:, 45:46], None, ALU.mult).then_inc(a_row, 1)
                else:
                    V.tensor_tensor(orow[:, m % 2, :].rearrange("p (j d) -> p j d", j=2),
                                    ps[:, 6, 0:P].rearrange("p (j d) -> p j d", j=2),
                                    st[:, 40 + a:42 + a].unsqueeze(2).broadcast_to((P, 2, HD)),
                                    ALU.mult).then_inc(a_row, 1)
            m = s - 3
            if 0 <= m < NI:
                qt, kind, c = ITEMS[m]
                dve.wait_ge(a_ot, m + 1)
                dst = act_t[:, 4 * kind + c, qt * P:(qt + 1) * P]
                if kind == 0:
                    V.tensor_scalar(dst, ps[:, 7, 0:P], PR("subln"), 1.0 - LAM_INIT, ALU.mult,
                                    ALU.mult).then_inc(a_cat, 1)
                else:
                    V.tensor_copy(dst, ps[:, 7, 0:P]).then_inc(a_cat, 1)
            if s < NI:
                qt, kind, c = ITEMS[s]
                n = (qt + 1) * P
                a = 2 * (s % 2)
                dve.wait_ge(a_exp, 2 * (s + 1))
                if s > 1:
                    dve.wait_ge(a_row, s - 1)
                rc = st[:, 40 + a:42 + a]
                if kind == 0:
                    link(V.reciprocal(rc, st[:, 36 + a:38 + a]))
                    S(V.tensor_scalar(Ex[:, s % 2, 0, 0:n], Ex[:, s % 2, 0, 0:n], rc[:, 0:1], None, ALU.mult))
                    link(V.tensor_tensor(rc[:, 1:2], rc[:, 1:2], st[:, 25:26], ALU.mult))
                    V.scalar_tensor_tensor(Ex[:, s % 2, 0, 0:n], Ex[:, s % 2, 1, 0:n], rc[:, 1:2],
                                           Ex[:, s % 2, 0, 0:n], ALU.mult, ALU.add).then_inc(a_p, 1)
                else:
                    V.reciprocal(rc, st[:, 36 + a:38 + a]).then_inc(a_p, 1)
        fence()
        S(V.memset(Qcur, 0.0))
        S(V.memset(ps[:, 6:8, 0:P], 0.0))
        S.done()
        for w in range(2):
            ins = V.tensor_copy(Qcur[:, w, :, 0:16], qS[w][:, 0, :, :])
        S(ins)
        S.done()
        dve.drain().then_inc(q_ready, 1)
        fence()

        steps0 = S.n
        PER = 6
        with dve.Fori(0, NB) as b:
            S.start(b * PER + steps0)

            def tev(g):
                nb = GROUPS[g][2]
                for c in (1, 3):
                    dve.wait_ge(t_done, b * 28 + 4 * (g - 1) + c + 1)
                    dve.wait_ge(s_mm, (b * 8 + (0 if g <= 2 else g - 1)) + 1)
                    V.tensor_copy(KTs[:, 4 * (g % 2) + c, 0:nb * P], ps[:, 1, 0:nb * P]).then_inc(te_dve, 1)

            def sw(g):
                dve.wait_ge(s_mm, b * 8 + g + 2)
                dve.wait_ge(pv_done, b * 8 + 1)
                at, n = (g - 5) * 512, GROUPS[g][2] * P
                V.scalar_tensor_tensor(S_w[:, at:at + n], ps[:, 2 + g % 2, 0:n], SCALE,
                                       C("old_win")[:, at:at + n], ALU.mult, ALU.add).then_inc(sw_ev, 1)

            tev(1)
            dve.wait_ge(s_mm, b * 8 + 2)
            dve.sem_inc(waited)
            dve.wait_ge(pv_done, b * 8 + 1)
            dve.sem_inc(waited)
            at = 56 - b * 8
            a0, _ = ccol["new_diff"]
            a1, _ = ccol["new_win"]
            S(V.tensor_tensor(S_d[:, PAST:PAST + TS], ps[:, 2, 0:TS], cst[:, bass.ds(at + a0, TS)], ALU.add))
            V.scalar_tensor_tensor(S_w[:, NWIN:NWIN + TS], ps[:, 2, TS:2 * TS], SCALE,
                                   cst[:, bass.ds(at + a1, TS)], ALU.mult, ALU.add).then_inc(sw_ev, 1)
            tev(2); tev(3); tev(4); tev(5)
            dve.wait_ge(sd_ev, b * 4 + 4)
            S.done()
            link(V.tensor_reduce(st[:, 48:49], S_d, AX.X, ALU.max))
            V.tensor_scalar(st[:, 48:49], st[:, 48:49], -SCALE, None, ALU.mult).then_inc(max_ready, 1)
            tev(6); sw(5); tev(7); sw(6); sw(7)
            dve.wait_ge(sw_ev, b * 4 + 5)
            link(V.tensor_reduce(st[:, 49:50], S_w, AX.X, ALU.max))
            V.tensor_scalar(st[:, 49:50], st[:, 49:50], -1.0, None, ALU.mult).then_inc(max_ready, 1)
            S(V.tensor_copy(Qcur[:, 0, :, 0:16], qS[0][:, bass.ds(b + 1, 1), :, :].rearrange("p a h c -> p (a h) c")))
            V.tensor_copy(Qcur[:, 1, :, 0:16],
                          qS[1][:, bass.ds(b + 1, 1), :, :].rearrange("p a h c -> p (a h) c")).then_inc(q_ready, 1)
            for k in (0, 2, 4, 6):
                w, blocks = CHUNKS[k]
                r = TS if k == 4 else P
                dve.wait_ge(pt_done, b * 8 + k + 1)
                V.tensor_copy((PT_w if w else PT_d)[0:r, blocks[0]:blocks[-1] + 1, :],
                              ps[0:r, 4, 0:len(blocks) * P].rearrange("p (n c) -> p n c", c=P)).then_inc(ptev_dve, 1)
            dve.wait_ge(exp_done, b * 2 + 2)
            link(V.reciprocal(st[:, 52:54], st[:, 50:52]))
            link(V.tensor_tensor(st[:, 52:53], st[:, 52:53], st[:, 24:25], ALU.mult))
            dve.wait_ge(pv_done, b * 8 + 9)
            dve.sem_inc(waited)
            for w in range(2):
                ins = V.tensor_scalar(O_all[w][:, bass.ds(b, 1), :].rearrange("p a d -> p (a d)"), ps[:, 6 + w, 0:P],
                                      st[:, 52 + w:53 + w], None, ALU.mult)
                ins.then_inc(o_ev, 1)
            assert S.k == PER, S.k
        S.start(steps0 + NB * PER)
        fence()
        dve.wait_ge(f_ev, 1)
        c32, q32 = comb[0:32], csq[0:32]
        link(V.tensor_tensor(q32, c32, c32, ALU.mult))
        link(V.tensor_reduce(st[0:32, 54:62], q32, AX.X, ALU.add))
        rstd(st[0:32, 54:62], st[0:32, 54:62], P)
        V.tensor_tensor(c32, c32, st[0:32, 54:62].unsqueeze(2).broadcast_to((32, NB, P)), ALU.mult).then_inc(f_ev, 1)
        dve.wait_ge(f_mm, 2)
        new = act_t[:, :, TP:T].rearrange("p k (b q) -> p k b q", b=NB)
        wide = ps[:, 3:5, :].rearrange("p a (b h c) -> p (a b) h c", b=4, h=4)
        for h in range(4):
            V.tensor_scalar(new[:, h], ps[:, 2, 0:256].rearrange("p (b h q) -> p b h q", b=NB, h=4)[:, :, h, :],
                            PR("subln"), 1.0 - LAM_INIT, ALU.mult, ALU.mult)
            for j in range(2):
                p = slice(64 * j, 64 * j + 64)
                V.tensor_copy(new[p, 4 + h], wide[p, :, h, 8 * j:8 * j + 8])
        fence()

        def residual(u):
            for i in range(2 * NT):
                n, t = divmod(i, NT)
                r = rows(t)
                dve.wait_ge(p_mm, u * 2 * NT + i + 1)
                xx = xt[0:r, t, n * 512:(n + 1) * 512]
                V.tensor_tensor(xx, xx, ps[0:r, i % 4, :], ALU.add).then_inc(p_ev, 1)

        dve.wait_ge(x_in, 64)
        residual(0)
        fence()

        def hb_step(m, n):
            dve.wait_ge(m["u"], n + 2)
            dve.wait_ge(m["silu"], n + 2)
            dve.wait_ge(m["ht"], n + 1)
            V.tensor_tensor(hb, sg, ps[:, 1, :], ALU.mult).then_inc(m["hb"], 1)

        def xgt_step(l, m, n, par_, free):
            dve.wait_ge(m["xt"], n + 1)
            if free is not None:
                dve.wait_ge(m["u"], free + 1)
            V.tensor_tensor(XgT[:, par_], ps[:, 2:4, :].rearrange("p a (k c) -> p (a k) c", k=4),
                            gain[:, 1 + 2 * l, :].unsqueeze(2).broadcast_to((P, KC, P)),
                            ALU.mult).then_inc(m["xgt"], 1)

        def layer_ffn(l):
            norm(1 + 2 * l)
            fence()
            link(V.memset(L, 0.0))
            dve.wait_ge(r_mm, 3 * l + 1)
            S(V.tensor_copy(L[:, 0:4, :], ps[:, 7, 0:144].rearrange("p (t e) -> p t e", t=4)))
            link(V.tensor_copy(L[0:TS, 4, :], ps[0:TS, 7, 144:180]))
            Lg, Le = L[:, :, 0:4], L[:, :, 4:36]

            def wide_(a, n):
                return a.unsqueeze(2).broadcast_to((P, NT, n))

            def first_hit(o, v, m, rank_, n, top_, tmp):
                link(V.tensor_tensor(tmp, v, wide_(m, n), ALU.is_equal))
                link(V.tensor_tensor(tmp, tmp, rank_.unsqueeze(1).broadcast_to((P, NT, n)), ALU.mult))
                link(V.tensor_reduce(top_, tmp, AX.X, ALU.max))
                link(V.tensor_tensor(o, tmp, wide_(top_, n), ALU.is_equal))

            link(V.tensor_reduce(g_max, Lg, AX.X, ALU.max))
            V.tensor_tensor(g_sub, Lg, wide_(g_max, 4), ALU.subtract).then_inc(r_ev, 1)
            first_hit(g_one, Lg, g_max, C("group_rank"), 4, g_top, g_hit)
            link(V.tensor_scalar(g_pen, g_one, 1.0, 1e30, ALU.subtract, ALU.mult))
            e4 = e_all.rearrange("p t (g e) -> p t g e", g=4)
            for g in range(4):
                S(V.tensor_tensor(e4[:, :, g, :], Le[:, :, 8 * g:8 * g + 8],
                                  g_one[:, :, g:g + 1].broadcast_to((P, NT, 8)), ALU.mult))
            S.done()
            for g in range(4):
                S(V.tensor_tensor(e4[:, :, g, :], e4[:, :, g, :],
                                  g_pen[:, :, g:g + 1].broadcast_to((P, NT, 8)), ALU.add))
            S.done()
            link(V.tensor_reduce(m_1, e_all, AX.X, ALU.max))
            first_hit(one[0], e_all, m_1, C("expert_rank"), NE, top, hit)
            link(V.scalar_tensor_tensor(e_all, one[0], -2e30, e_all, ALU.mult, ALU.add))
            link(V.tensor_reduce(m_2, e_all, AX.X, ALU.max))
            V.tensor_tensor(e_dif, m_2, m_1, ALU.subtract).then_inc(r_ev, 1)
            first_hit(one[1], e_all, m_2, C("expert_rank"), NE, top, hit)
            link(V.tensor_tensor(both, one[0], one[1], ALU.add))
            V.tensor_tensor(both, both, wide_(C("valid"), NE), ALU.mult).then_inc(r_ev, 1)
            dve.wait_ge(r_exp, 2 * l + 1)
            link(V.tensor_reduce(g_sum, g_exp, AX.X, ALU.add))
            dve.wait_ge(r_exp, 2 * l + 2)
            link(V.scalar_tensor_tensor(g_sum, e_exp, 1.0, g_sum, ALU.add, ALU.mult))
            link(V.reciprocal(wts[:, 0], g_sum))
            link(V.tensor_tensor(wts[:, 1], wts[:, 0], e_exp, ALU.mult))
            dve.wait_ge(r_mm, 3 * l + 2)
            S(V.tensor_copy(rank, ps[:, 6, 0:160].rearrange("p (t e) -> p t e", t=NT)))
            S(V.tensor_copy(count, ps[:, 6, 160:192]))
            S.done()
            link(V.tensor_scalar(more, count, float(P), None, ALU.is_gt))
            for i in range(2, 5):
                link(V.scalar_tensor_tensor(more, count, float(P * i), more, ALU.is_gt, ALU.add))
            src, dst = more, pre_a
            for k in (1, 2, 4, 8, 16):
                S(V.tensor_copy(dst[:, 0:k], src[:, 0:k]))
                link(V.tensor_tensor(dst[:, k:NE], src[:, k:NE], src[:, 0:NE - k], ALU.add))
                src, dst = dst, (pre_b if dst is pre_a else pre_a)
            incl = src
            link(V.tensor_tensor(shift_f, incl, more, ALU.subtract))
            link(V.scalar_tensor_tensor(shift_f, shift_f, float(P), C("expert_shift"), ALU.mult, ALU.add))
            link(V.scalar_tensor_tensor(slot_f, rank, float(P), shift_f.unsqueeze(1).broadcast_to((P, NT, NE)),
                                        ALU.is_ge, ALU.mult))
            link(V.tensor_tensor(slot_f, slot_f, rank, ALU.add))
            link(V.tensor_tensor(slot_f, slot_f, C("expert_base").unsqueeze(1).broadcast_to((P, NT, NE)), ALU.add))
            for s in range(2):
                link(V.tensor_tensor(pick, slot_f, one[s], ALU.mult))
                link(V.tensor_reduce(slots[:, s], pick, AX.X, ALU.add))
            V.tensor_copy(slotI, slots.rearrange("p s t -> p (s t)")).then_inc(r_slot, 1)
            r0 = slice(0, 1)
            link(V.tensor_tensor(x_hit[r0], incl[r0].unsqueeze(1).broadcast_to((1, NX, NE)),
                                 C("extra_no")[r0].unsqueeze(2).broadcast_to((1, NX, NE)), ALU.is_le))
            link(V.tensor_reduce(x_exp[r0], x_hit[r0], AX.X, ALU.add))
            link(V.tensor_scalar(x_exp[r0], x_exp[r0], float(NE - 1), None, ALU.min))
            link(V.tensor_copy(sti[r0, 88:96], x_exp[r0]))
            link(V.tensor_copy(sti[r0, 96:97], incl[r0, NE - 1:NE]))
            dve.wait_ge(r_mm, 3 * l + 3)
            link(V.tensor_copy(sti[:, 0:80], ps[:, 5, 0:80]))
            fence()

            m, mx = moe[2 * l], moe[2 * l + 1]
            xgt_step(l, m, 0, 0, None)
            hb_after(m, l)
            fence()

        def hb_after(m, l):
            mx = moe[2 * l + 1]
            hb_step(m, 0)
            xgt_step(l, m, 1, 1, None)
            with dve.Fori(0, NE // 2 - 1) as j:
                hb_step(m, 2 * j + 1)
                xgt_step(l, m, 2 * j + 2, 0, 2 * j + 1)
                hb_step(m, 2 * j + 2)
                xgt_step(l, m, 2 * j + 3, 1, 2 * j + 2)
            hb_step(m, NE - 1)
            n_extra = dve.value_load(sti[0:1, 96:97], min_val=0, max_val=NX)
            with dve.Fori(0, NX) as j:
                with dve.If(n_extra > j):
                    xgt_step(l, mx, j, 0, j)
                    hb_step(mx, j)
            for t in range(NT):
                r = rows(t)
                dve.wait_ge(y_back[t % 2], 16 * (l * (3 - t % 2) + t // 2 + 1))
                link(V.scalar_tensor_tensor(xt[0:r, t], y01[0:r, t % 2, 0], wts[0:r, 0, t:t + 1], xt[0:r, t],
                                            ALU.mult, ALU.add))
                V.scalar_tensor_tensor(xt[0:r, t], y01[0:r, t % 2, 1], wts[0:r, 1, t:t + 1], xt[0:r, t],
                                       ALU.mult, ALU.add).then_inc(y_used, 1)

        layer_ffn(0)
        norm(2)
        fence()

        wdw = PR("w_dw").rearrange("p (c j) -> p c j", c=KC)
        us = u_ext[:, :, CK - 1 + TP:].rearrange("p c (b w) -> p c b w", b=NB)
        dve.wait_ge(state_in, 16 * KC)
        for ch in range(KC):
            bank = 4 * (ch % 2)
            ba = PR("b_pw1")[:, ch:ch + 1]
            dve.wait_ge(pw_sig, ch + 1)
            S(V.scalar_tensor_tensor(u_ext[:, ch, CK - 1:CK - 1 + HALF], ps[:, bank, 0:HALF], ba,
                                     sig[:, ch % 2, 0:HALF], ALU.add, ALU.mult))
            rest = TP - HALF
            S(V.scalar_tensor_tensor(u_ext[:, ch, CK - 1 + HALF:CK - 1 + TP], ps[:, bank + 1, 0:rest], ba,
                                     sig[:, ch % 2, HALF:TP], ALU.add, ALU.mult))
            V.scalar_tensor_tensor(us[:, ch, :, CK - 1:], ps[:, bank + 1, rest:HALF].rearrange("p (b q) -> p b q", b=NB),
                                   ba, sig[:, ch % 2, TP:T].rearrange("p (b q) -> p b q", b=NB),
                                   ALU.add, ALU.mult).then_inc(glu, 1)
            dve.wait_ge(glu, ch + 1)
            S.done()
            for j in range(CK):
                for o, i in ((cc[:, ch, 0:TP], u_ext[:, ch, j:j + TP]),
                             (cc[:, ch, TP:T].rearrange("p (b q) -> p b q", b=NB), us[:, ch, :, j:j + NQ])):
                    if j == 0:
                        S(V.tensor_scalar(o, i, wdw[:, ch, 0:1], PR("b_dw")[:, ch:ch + 1], ALU.mult, ALU.add))
                    else:
                        dve.wait_ge(dve_step, S.n - 1)
                        S(V.scalar_tensor_tensor(o, i, wdw[:, ch, j:j + 1], o, ALU.mult, ALU.add))
        fence()

        dve.wait_ge(mean_mm, 1)
        mean, inv = mr[:, 0, :], mr[:, 1, :]
        halves = "p (h n) -> p h n"
        link(V.tensor_scalar(mean.rearrange(halves, h=2), ps[:, 0:2, 0:HALF], 1.0 / D, None, ALU.mult))
        V.tensor_tensor(cc, cc, mean.unsqueeze(1).broadcast_to((P, KC, T)), ALU.subtract).then_inc(centred, 1)
        dve.wait_ge(var_mm, KC)
        V.tensor_scalar(inv.rearrange(halves, h=2), ps[:, 2:4, 0:HALF], 1.0 / D, EPS, ALU.mult, ALU.add).then_inc(var_ready, 1)
        dve.wait_ge(root, 1)
        link(V.reciprocal(inv, inv))
        dve.wait_ge(centred, 1)
        for ch in range(KC):
            V.tensor_tensor(cc[:, ch], cc[:, ch], inv, ALU.mult).then_inc(normed, 1)
        fence()
        residual(1)
        fence()
        layer_ffn(1)

        dve.wait_ge(norm_sq, 5)
        rstd(st[:, 5:10], st[:, 0:5], D)
        dve.wait_ge(x_in, 80)
        for t in range(NT):
            r = rows(t)
            if t >= 2:
                dve.wait_ge(rows_out2[t % 2], 16 * (2 * (3 - t % 2) + t // 2))
            V.scalar_tensor_tensor(xn[0:r, t % 2, :], xt[0:r, t, :], st[0:r, 5 + t:6 + t], gf[0:r, :],
                                   ALU.mult, ALU.mult).then_inc(norm_rows, 1)

    @block.tensor
    def _(pe):
        fence = Fence(pe, "pe")
        mm = nc.tensor.matmul

        def turn(o, i, n=P):
            return nc.tensor.transpose(o, i, ident[0:n, 0:n])

        def norm(u):
            for t in range(NT):
                r = rows(t)
                pe.wait_ge(norm_rows, NT * u + t + 1)
                if t >= 2:
                    pe.wait_ge(norm_ev, NT * u + t - 1)
                for k in range(KC):
                    ins = turn(ps[:, 2 * (t % 2) + k // 4, (k % 4) * P:(k % 4) * P + r],
                               xn[0:r, t % 2, k * P:(k + 1) * P], r)
                ins.then_inc(norm_tr, 1)

        pe.wait_ge(consts_in, 48)
        pe.wait_ge(lam_ready, 1)
        mm(ps[:, 7, 0:2], ones, st[:, 22:24], start=True, stop=True).then_inc(lam_mm, 1)
        norm(0)
        fence()

        def z_turn(n, t, k):
            r = rows(t)
            pe.wait_ge(z_rope, k + 1)
            if k > 1:
                pe.wait_ge(z_tev, k - 1)
            for h in range(4):
                ins = turn(ps[:, k % 2, h * P:h * P + r], zrow[0:r, k % 4, h * P:(h + 1) * P], r)
            ins.then_inc(z_tr, 1)

        prev, i_z = [], 0
        for n in range(6):
            pe.wait_ge(loaded[n], 16)
            for t in range(NT):
                r = rows(t)
                if i_z > 3:
                    pe.wait_ge(z_copy, i_z - 3)
                for k in range(KC):
                    ins = mm(ps[0:r, 4 + i_z % 4, :], act_t[:, k, t * P:t * P + r], slot(n, 8)[:, k, :],
                             start=(k == 0), stop=(k == KC - 1))
                ins.then_inc(z_mm, 1)
                i_z += 1
                if prev:
                    z_turn(*prev.pop())
                if n in qtab:
                    prev.append((n, t, qtab[n] * NT + t))
        if prev:
            z_turn(*prev.pop())
        fence()

        for s in range(NI + 3):
            if s < NI:
                qt, kind, c = ITEMS[s]
                n = (qt + 1) * P
                if 2 * (s - 1) > 0:
                    pe.wait_ge(a_exp, 2 * (s - 1))
                for j in range(2):
                    p = slice(64 * j, 64 * j + 64)
                    ins = mm(ps[:, 2 * (s % 2) + j, 0:n], qT[kind][p, c, qt * P:(qt + 1) * P],
                             kT[kind][p, c, 0:n], start=True, stop=True)
                ins.then_inc(a_s, 1)
            m = s - 2
            if 0 <= m < NI:
                qt, kind, c = ITEMS[m]
                pe.wait_ge(a_ptev, m + 1)
                if m > 0:
                    pe.wait_ge(a_row, m)
                nj = 2 if kind else 1
                for j in range(nj):
                    w = P // nj
                    for kb in range(qt + 1):
                        ins = mm(ps[:, 6, j * w:(j + 1) * w], PTsb[:, m % 2, j, kb * P:(kb + 1) * P],
                                 vP[kind][:, kb, c * P + j * w:c * P + (j + 1) * w],
                                 start=(kb == 0), stop=(kb == qt))
                ins.then_inc(a_o, 1)
            m = s - 1
            if 0 <= m < NI:
                qt, kind, c = ITEMS[m]
                pe.wait_ge(a_p, m + 1)
                if m > 0:
                    pe.wait_ge(a_ptev, m)
                for j in range(2 if kind else 1):
                    for kb in range(qt + 1):
                        ins = turn(ps[:, 4 + j, kb * P:(kb + 1) * P], Ex[:, m % 2, j, kb * P:(kb + 1) * P])
                ins.then_inc(a_t, 1)
            m = s - 3
            if 0 <= m < NI:
                pe.wait_ge(a_row, m + 1)
                if m > 0:
                    pe.wait_ge(a_cat, m)
                turn(ps[:, 7, 0:P], orow[:, m % 2, :]).then_inc(a_ot, 1)
        fence()
        fence()

        with pe.Fori(0, NB) as b:
            def turn_keys(g):
                s, first, nb, _ = GROUPS[g]
                if g in (1, 3, 5):
                    pe.wait_ge(loaded[s], b * PER_BATCH[s] + 16 + PER_BATCH[s])
                if g == 7:
                    pe.wait_ge(aux_in[0], b * 16 + 16)
                for c in range(4):
                    u = 4 * (g - 1) + c
                    pe.wait_ge((te_act, te_dve)[c % 2], b * 14 + u // 2 + 1)
                    for i in range(nb):
                        blk = aux[:, i, c * P:(c + 1) * P] if s is None else slot(s, 8)[:, first + i, c * P:(c + 1) * P]
                        ins = turn(ps[:, c % 2, i * P:(i + 1) * P], blk)
                    ins.then_inc(t_done, 1)

            def scores(g):
                bank = 2 + g % 2
                if g in (0, 1):
                    pe.wait_ge(sw_ev, b * 4 + 1)
                elif g in (2, 7):
                    pe.wait_ge(sw_ev, (b * 4 + (1 if g == 2 else 2)) + 1)
                else:
                    pe.wait_ge(sd_ev, b * 4 + g - 2)
                if g == 0:
                    pe.wait_ge(q_ready, b + 1)
                    for w in range(2):
                        for c in range(4):
                            ins = mm(ps[32 * c:32 * c + 32, bank, w * TS:(w + 1) * TS], Qcur[:, w, c, :],
                                     kS[w][:, c, :], start=True, stop=True)
                else:
                    pe.wait_ge(te_act, b * 14 + 2 * g + 1)
                    pe.wait_ge(te_dve, b * 14 + 2 * g + 1)
                    n = GROUPS[g][2] * P
                    for c in range(4):
                        ins = mm(ps[32 * c:32 * c + 32, bank, 0:n], Qcur[:, int(g > 4), c, :],
                                 KTs[:, 4 * (g % 2) + c, 0:n], start=True, stop=True)
                ins.then_inc(s_mm, 1)

            def turn_probs(k):
                w, blocks = CHUNKS[k]
                if k in (0, 5):
                    pe.wait_ge(exp_done, b * 2 + w + 1)
                    pe.sem_inc(waited)
                if k % 2:
                    pe.wait_ge(ptev_act, b * 5 + (k - 1) // 2 + 1)
                    pe.sem_inc(waited)
                else:
                    pe.wait_ge(ptev_dve, b * 4 + k // 2 + 1)
                    pe.sem_inc(waited)
                for i, blk in enumerate(blocks):
                    src, new = (S_w, 10) if w else (S_d, 16)
                    n = TS if blk == new else P
                    ins = turn(ps[0:n, 4 + k % 2, i * P:(i + 1) * P], src[:, blk * P:blk * P + n])
                ins.then_inc(pt_done, 1)

            def products(k):
                w, blocks = CHUNKS[k]
                if k % 2:
                    pe.wait_ge(ptev_act, (b * 5 + ((k - 1) // 2 + 1 if k < 7 else 5)) + 1)
                    pe.sem_inc(waited)
                else:
                    pe.wait_ge(ptev_dve, b * 4 + k // 2 + 2)
                    pe.sem_inc(waited)
                for s, at in ((2, 0), (3, 2), (5, 5)):
                    if k == at:
                        pe.wait_ge(loaded[s], b * PER_BATCH[s] + 16 + PER_BATCH[s])
                if k == 7:
                    pe.wait_ge(aux_in[1], b * 16 + 16)
                if k in (0, 5):
                    pe.wait_ge(o_ev, b * 2 + 1)
                for blk in blocks:
                    r = P
                    if w:
                        if blk < 8:
                            v = slot(5, 8)[:, blk, :]
                        elif blk < 10:
                            v = aux[:, 2 + blk - 8, :]
                        else:
                            v, r = vS[1][0:TS], TS
                    elif blk < 16:
                        v = slot(2 + blk // 8, 8)[:, blk % 8, :]
                    else:
                        v, r = vS[0][0:TS], TS
                    pt = PT_w if w else PT_d
                    for c in range(4):
                        ins = mm(ps[32 * c:32 * c + 32, 6 + w, 0:P], pt[0:r, blk, 32 * c:32 * c + 32],
                                 v[:, c * P:(c + 1) * P], start=(blk == 0), stop=(blk == (10 if w else 16)))
                ins.then_inc(pv_done, 1)

            turn_keys(1); scores(0)
            for g in range(2, 8):
                turn_keys(g)
                scores(g - 1)
            scores(7)
            turn_probs(0)
            for k in range(8):
                if k < 7:
                    turn_probs(k + 1)
                products(k)
        fence()

        for i in range(2):
            ins = mm(ps[0:32, i, :], C("pair"), O_all[0][:, 4 * i:4 * i + 4, :].rearrange("p b d -> p (b d)"),
                     start=True, stop=True)
        ins.then_inc(f_mm, 1)
        for b in range(NB):
            turn(ps[:, 3 + b // 4, (b % 4) * P:(b % 4 + 1) * P], O_all[1][:, b, :])
        pe.wait_ge(f_ev, 2)
        for b in range(NB):
            ins = turn(ps[:, 2, 32 * b:32 * b + 32], comb[0:32, b, :], 32)
        ins.then_inc(f_mm, 1)
        fence()

        def project(u, src, done):
            for i in range(2 * NT):
                n, t = divmod(i, NT)
                r = rows(t)
                if t == 0:
                    pe.wait_ge(loaded[n], done[n])
                if i >= 4:
                    pe.wait_ge(p_ev, u * 2 * NT + i - 3)
                if u:
                    mm(ps[0:r, i % 4, :], ones[0:1, 0:r], brow[:, n * 512:(n + 1) * 512], start=True, stop=False)
                for k in range(KC):
                    ins = mm(ps[0:r, i % 4, :], src[:, k, t * P:t * P + r], slot(n, 8)[:, k, :],
                             start=(k == 0 and not u), stop=(k == KC - 1))
                ins.then_inc(p_mm, 1)

        project(0, act_t, [AFTER_BATCH[s] + 16 for s in range(2)])
        fence()

        def xt_step(m, n, par_, gathered):
            pe.wait_ge(m[f"gathered{par_}"], gathered)
            pe.wait_ge(m["xgt"], n + 1)
            for k in range(KC):
                ins = turn(ps[:, 2 + k // 4, (k % 4) * P:(k % 4 + 1) * P], Xg[:, par_, k * P:(k + 1) * P])
            ins.then_inc(m["xt"], 1)

        def gu_step(m, n, par_, s, weights):
            pe.wait_ge(m["xgt"], n + 2)
            for i, (name, used) in enumerate((("g", "silu"), ("u", "hb"))):
                pe.wait_ge(m[used], n + 1)
                weights(i)
                for k in range(KC):
                    ins = mm(ps[:, i, :], XgT[:, par_, k, :], slot(s[i], 8)[:, k, :], start=(k == 0), stop=(k == KC - 1))
                ins.then_inc(m[name], 1)

        def down_step(m, n, s, weights):
            pe.wait_ge(m["hb"], n + 2)
            pe.wait_ge(m["hbt"], n + 1)
            for k in range(4):
                ins = turn(ps[:, 4, k * P:(k + 1) * P], hb[:, k * P:(k + 1) * P])
            ins.then_inc(m["ht"], 1)
            weights(2)
            pe.wait_ge(m["hbt"], n + 2)
            for h in range(2):
                pe.wait_ge(m["yev"], (2 * n if h == 0 else 2 * n) + 1)
                for k in range(4):
                    ins = mm(ps[:, 5 + h, :], hbT[:, k, :], slot(s, 4)[:, k, h * 512:(h + 1) * 512],
                             start=(k == 0), stop=(k == 3))
                ins.then_inc(m["y"], 1)

        def layer_ffn(l):
            norm(1 + 2 * l)
            fence()
            for t in range(NT):
                r = rows(t)
                for k in range(KC):
                    ins = mm(ps[0:r, 7, t * 36:(t + 1) * 36], act_t[:, k, t * P:t * P + r], router[:, l, k, :],
                             start=(k == 0), stop=(k == KC - 1))
            ins.then_inc(r_mm, 1)
            pe.wait_ge(r_ev, 3 * l + 3)
            for t in range(NT):
                for i in range(t + 1):
                    mm(ps[:, 6, t * NE:(t + 1) * NE], C("before") if i == t else ones, both[:, i, :],
                       start=(i == 0), stop=(i == t))
            for i in range(NT):
                ins = mm(ps[:, 6, 160:192], ones, both[:, i, :], start=(i == 0), stop=(i == NT - 1))
            ins.then_inc(r_mm, 1)
            pe.wait_ge(table_io, 32 + (l + 1) * 16 * 11)
            for i in range(2):
                ins = turn(ps[:, 5, 40 * i:40 * i + 40], tab[:, :, i], NE + NX)
            ins.then_inc(r_mm, 1)
            fence()

            m, mx = moe[2 * l], moe[2 * l + 1]

            def weights(par_, turns):
                def w(kind):
                    s = eslots(par_)[kind]
                    pe.wait_ge(loaded[s], turns * 16 + moe_base(l, s))
                return w

            xt_step(m, 0, 0, 16)
            gu_step(m, 0, 0, eslots(0), weights(0, 1))
            xt_step(m, 1, 1, 16)
            with pe.Fori(0, NE // 2 - 1) as j:
                gu_step(m, 2 * j + 1, 1, eslots(1), weights(1, j + 1))
                down_step(m, 2 * j, eslots(0)[2], weights(0, j + 1))
                xt_step(m, 2 * j + 2, 0, j * 16 + 32)
                gu_step(m, 2 * j + 2, 0, eslots(0), weights(0, j + 2))
                down_step(m, 2 * j + 1, eslots(1)[2], weights(1, j + 1))
                xt_step(m, 2 * j + 3, 1, j * 16 + 32)
            gu_step(m, NE - 1, 1, eslots(1), weights(1, NE // 2))
            down_step(m, NE - 2, eslots(0)[2], weights(0, NE // 2))
            down_step(m, NE - 1, eslots(1)[2], weights(1, NE // 2))
            pe.wait_ge(m["yev"], 2 * NE + 1)
            n_extra = pe.value_load(sti[0:1, 96:97], min_val=0, max_val=NX)
            with pe.Fori(0, NX) as j:
                with pe.If(n_extra > j):
                    def x_weights(kind):
                        pe.wait_ge(x_loaded[l], j * 48 + 48)
                    xt_step(mx, j, 0, j * 16 + 16)
                    gu_step(mx, j, 0, (2, 3), x_weights)
                    down_step(mx, j, 4, x_weights)
            fence()

        layer_ffn(0)
        norm(2)
        fence()

        for ch in range(KC):
            first = 2 + 2 * (ch // 4)
            if ch % 4 == 0:
                for s in (first, first + 1):
                    pe.wait_ge(loaded[s], moe_base(1, s))
            if ch > 1:
                pe.wait_ge(glu, ch - 1)
            for i in range(2):
                for h in range(2):
                    for k in range(KC):
                        ins = mm(ps[:, 4 * (ch % 2) + 2 * i + h, 0:HALF],
                                 slot(first + i, 8)[:, k, (ch % 4) * P:(ch % 4 + 1) * P],
                                 act_t[:, k, h * HALF:(h + 1) * HALF], start=(k == 0), stop=(k == KC - 1))
            ins.then_inc(pw_mm, 1)
        pe.wait_ge(glu, KC)
        last = CK - 1 + TP - (CK - 1)
        for ch in range(KC):
            c0 = (ch % 4) * P
            turn(ps[0:CK - 1, ch // 4, c0:c0 + P], u_ext[:, ch, last:last + CK - 1])
            if ch == 0:
                pe.wait_ge(cv_new, 1)
            ins = turn(ps[0:TS, 2 + ch // 4, c0:c0 + P], act_t[:, ch, 0:TS])
        ins.then_inc(cv_tr, 1)
        fence()

        for h in range(2):
            for ch in range(KC):
                ins = mm(ps[:, h, 0:HALF], ones, cc[:, ch, h * HALF:(h + 1) * HALF], start=(ch == 0), stop=(ch == KC - 1))
        ins.then_inc(mean_mm, 1)
        for ch in range(KC):
            pe.wait_ge(squared, ch + 1)
            for h in range(2):
                ins = mm(ps[:, 2 + h, 0:HALF], ones, sig[:, ch % 2, h * HALF:(h + 1) * HALF],
                         start=(ch == 0), stop=(ch == KC - 1))
            ins.then_inc(var_mm, 1)
        fence()
        pe.wait_ge(state_in, 16 * KC + 16)
        project(1, cc, [moe_base(1, s) for s in range(2)])
        fence()
        layer_ffn(1)

    @block.gpsimd
    def _(pool):
        G = Steps(pool, pool_step)
        fence = Fence(pool, "pool")
        IDX = bass.IndirectOffsetOnAxis

        def load_x(src_p, src_s):
            pool.dma_start(xt[:, 0:4, :], src_p.rearrange("(t p) d -> p t d", p=P)).then_inc(x_in, 16)
            pool.dma_start(xt[0:TS, 4, :], src_s).then_inc(x_in, 16)

        for q in with_lead:
            pool.sem_inc(q)
        load_x(x_prompt, x_sample)
        far = B(0, 256)[0:NE + NX]
        G(nc.gpsimd.memset(far, FAR))
        G.done()
        for l in range(2):
            pool.dma_start(table[l].rearrange("(b s) c -> b (s c)", s=P), far).then_inc(table_io, 16)
        pool.wait_ge(table_io, 32)
        fence()

        outs = {1: (nkd_p, nkd_s), 2: (nvd_p, nvd_s), 4: (nwk_p, nwk_s), 5: (nwv_p, nwv_s)}
        n_v = 0
        for n in range(6):
            for t in range(NT):
                if n not in outs:
                    continue
                dst = outs[n][0][t * P:(t + 1) * P] if t < 4 else outs[n][1]
                if t == 4 and n > 3:
                    dst = dst[:, PAST - NQ:PAST, :]
                if n in qtab:
                    k = qtab[n] * NT + t
                    pool.wait_ge(z_rope, k + 1)
                    src = zrow[0:rows(t), k % 4, :]
                    pool.dma_start(dst, src).then_inc(z_out[k % 4], 16)
                else:
                    pool.wait_ge(z_copy, n * NT + t + 1)
                    src = vP[n // 4][:, t, :] if t < 4 else vS[n // 4][0:TS, :]
                    pool.dma_start(dst, src).then_inc(out_done, 16)
                    n_v += 1
        for i in range(4):
            pool.wait_ge(z_out[i], 16 * stores_before(20 + i))
        pool.wait_ge(out_done, 16 * n_v)
        for _ in range(5):
            fence()
        load_x(x_prompt, x_sample)
        fence()

        def layer_ffn(l):
            for t in range(NT):
                r = rows(t)
                pool.wait_ge(norm_rows, NT * (1 + 2 * l) + t + 1)
                pool.dma_start(h_rows[l][t * P:t * P + r], xn[0:r, t % 2, :]).then_inc(rows_out2[t % 2], 16)
            for i in range(2):
                pool.wait_ge(rows_out2[i], 16 * (3 - i) * (l + 1))
            fence()
            pool.wait_ge(r_slot, l + 1)
            for s in range(2):
                for t in range(NT):
                    r = rows(t)
                    pool.indirect_dma_start(table[l], IDX(slotI[0:r, s * NT + t:s * NT + t + 1], 0),
                                            codes[0:r, s, t, :], None,
                                            bounds_check=(NE + NX) * P - 1, oob_is_err=False).then_inc(table_io, 16)
            pool.wait_ge(table_io, 32 + l * 16 * 11 + 160)
            pool.dma_start(tab.rearrange("b s c -> b (s c)"),
                           table[l].rearrange("(b s) c -> b (s c)", s=P)).then_inc(table_io, 16)
            fence()

            m, mx = moe[2 * l], moe[2 * l + 1]
            G(nc.gpsimd.memset(Xg, 0.0))
            G.done()

            def gather_dma(mm_, par_):
                pool.indirect_dma_start(Xg[:, par_, :], None, h_rows[l], IDX(tokS[:, par_:par_ + 1], 0),
                                        bounds_check=T - 1, oob_is_err=False).then_inc(mm_[f"gathered{par_}"], 16)

            def scatter_dma(mm_, par_):
                pool.indirect_dma_start(y_rows[l], IDX(codeS[:, par_:par_ + 1], 0), Y[:, par_, :], None,
                                        bounds_check=2 * T - 1, oob_is_err=False).then_inc(mm_[f"scattered{par_}"], 16)

            def do_gather(mm_, xt_needed, par_, block_, ready):
                if xt_needed is not None:
                    pool.wait_ge(mm_["xt"], xt_needed)
                    pool.sem_inc(waited)
                pool.tensor_copy(tokS[:, par_:par_ + 1], tokI[:, block_]).then_inc(tok_ready, 1)
                pool.wait_ge(tok_ready, ready)
                pool.sem_inc(waited)
                gather_dma(mm_, par_)

            def do_scatter(mm_, n, par_, block_, used, ready):
                pool.wait_ge(mm_["yev"], 2 * n + 3)
                pool.sem_inc(waited)
                if used is not None:
                    pool.wait_ge(mm_[f"scattered{par_}"], used)
                    pool.sem_inc(waited)
                pool.tensor_copy(codeS[:, par_:par_ + 1], codeI[:, block_]).then_inc(code_ready, 1)
                pool.wait_ge(code_ready, ready)
                pool.sem_inc(waited)
                scatter_dma(mm_, par_)

            base = l * NE
            for par_ in range(2):
                do_gather(m, None, par_, slice(par_, par_ + 1), base + par_ + 1)
            for par_ in range(2):
                do_gather(m, par_ + 1, par_, slice(2 + par_, 3 + par_), base + 3 + par_)
                do_scatter(m, par_, par_, slice(par_, par_ + 1), None, base + 1 + par_)
            with pool.Fori(1, NE // 2 - 1) as j:
                for par_ in range(2):
                    do_gather(m, 2 * j + par_ + 1, par_, bass.ds(2 * j + 2 + par_, 1), 2 * j + (base + 3 + par_))
                    do_scatter(m, 2 * j + par_, par_, bass.ds(2 * j + par_, 1), j * 16, 2 * j + (base + 1 + par_))
            for par_ in range(2):
                n = NE - 2 + par_
                do_scatter(m, n, par_, slice(n, n + 1), 15 * 16, base + n + 1)
            for par_ in range(2):
                pool.wait_ge(m[f"scattered{par_}"], 16 * 16)
                pool.sem_inc(waited)
            n_extra = pool.value_load(sti[0:1, 96:97], min_val=0, max_val=NX)
            with pool.Fori(0, NX) as j:
                with pool.If(n_extra > j):
                    pool.tensor_copy(tokS[:, 0:1], tokI[:, bass.ds(j + NE, 1)]).then_inc(x_ready[l], 1)
                    pool.wait_ge(x_ready[l], 2 * j + 1)
                    pool.sem_inc(waited)
                    gather_dma(mx, 0)
                    pool.wait_ge(mx["yev"], 2 * j + 3)
                    pool.sem_inc(waited)
                    pool.tensor_copy(codeS[:, 0:1], codeI[:, bass.ds(j + NE, 1)]).then_inc(x_ready[l], 1)
                    pool.wait_ge(x_ready[l], 2 * j + 2)
                    pool.sem_inc(waited)
                    scatter_dma(mx, 0)
                    pool.wait_ge(mx["scattered0"], j * 16 + 16)
                    pool.sem_inc(waited)
            for t in range(NT):
                r = rows(t)
                if t >= 2:
                    pool.wait_ge(y_used, NT * l + t - 1)
                pool.dma_start(y01[0:r, t % 2], y_rows[l][2 * P * t:2 * P * t + 2 * r].rearrange("(p s) d -> p s d", s=2)
                               ).then_inc(y_back[t % 2], 16)
            fence()

        layer_ffn(0)
        fence()
        G(nc.gpsimd.memset(u_ext[:, :, 0:CK - 1], 0.0))
        G.done()
        for ch in range(KC):
            pool.dma_start(u_ext[:, ch, CK - 1 + TP:].rearrange("p (b w) -> p b w", b=NB)[:, :, 0:CK - 1],
                           st_cols[ch]).then_inc(state_in, 16)
        pool.wait_ge(cv_ev, 2)
        pool.dma_start(ncv_p, crow_p).then_inc(out_done, 16)
        pool.dma_start(ncv_s[:, CK - 1 - NQ:, :], crow_s).then_inc(out_done, 16)
        pool.wait_ge(out_done, 16 * (n_v + 2))
        fence()
        pool.dma_start(brow, vecs[0:1, :]).then_inc(state_in, 16)
        fence()
        fence()
        layer_ffn(1)
        pool.dma_start(gf, vecs[1:2, :].broadcast_to((P, D))).then_inc(x_in, 16)
        for t in range(NT):
            r = rows(t)
            pool.wait_ge(norm_rows, 4 * NT + t + 1)
            dst = y_p[t * P:(t + 1) * P] if t < 4 else y_s
            pool.dma_start(dst, xn[0:r, t % 2, :]).then_inc(rows_out2[t % 2], 16)
        for i in range(2):
            pool.wait_ge(rows_out2[i], 16 * (3 - i) * 3)

    ctx.close()


_OUTS = [(1, 512, 1024), (8, 8, 1024), (1, 1, 512, 4, 128), (1, 1, 512, 4, 128), (1, 8, 8, 4, 128), (1, 8, 8, 4, 128),
         (1, 1, 512, 8, 64), (1, 1, 512, 8, 64), (1, 8, 2048, 8, 64), (1, 8, 2048, 8, 64), (1, 1, 30, 1024), (1, 8, 30, 1024)]
_VIEWS = [(512, 1024), (64, 1024), (512, 512), (512, 512), (64, 512), (64, 512),
          (512, 512), (512, 512), (8, 2048, 512), (8, 2048, 512), (30, 1024), (8, 30, 1024)]


def kernel(**inputs):
    import numpy as _np
    import concourse.bacc as _bacc
    from concourse import mybir as _mybir
    from concourse.bass_utils import run_bass_kernel_spmd as _run

    a = {k: _np.asarray(v) for k, v in inputs.items()}

    def cols(v, n):
        return v.reshape(n, P).T

    def pad(v):
        return _np.concatenate([v.reshape(-1), _np.zeros(P - HD, v.dtype)]).reshape(P, 1)

    routers = []
    for l in range(2):
        w = _np.concatenate([a["w_router_group"][l], a["w_router_expert"][l].transpose(1, 0, 2).reshape(D, NE)], 1)
        routers.append(w.reshape(KC, P, 36).transpose(1, 0, 2).reshape(P, -1))
    params = _np.concatenate(
        [cols(a["norm_mix"][0], KC), cols(a["norm_ffn"][0], KC), cols(a["norm_mix"][1], KC), cols(a["norm_ffn"][1], KC),
         a["subln_gain"].reshape(P, 1),
         a["w_dw"][0].T.reshape(KC, P, CK).transpose(1, 0, 2).reshape(P, -1),
         cols(a["b_dw"][0], KC), cols(a["ln_conv_gain"][0], KC), cols(a["ln_conv_bias"][0], KC),
         cols(a["b_pw1"][0], 16), *routers,
         pad(a["lambda_q1"]), pad(a["lambda_k1"]), pad(a["lambda_q2"]), pad(a["lambda_k2"])], 1)
    st = a["state_conv"][0]
    arrays = [
        a["x_prompt"][0], a["x_sample"].reshape(TS, D),
        a["cache_k_diff"][0].reshape(-1, PAGE, 512), a["cache_v_diff"][0].reshape(-1, PAGE, 512),
        a["cache_win_k"][0].reshape(NB, PAST, 512), a["cache_win_v"][0].reshape(NB, PAST, 512),
        st, st.transpose(2, 0, 1).reshape(KC, P, NB, CK - 1),
        a["page_table"].reshape(1, -1), a["w_in_attn"][0], a["w_out_attn"][0], a["w_pw1"][0], a["w_pw2"][0],
        a["w_exp_gate"].reshape(-1, D, F), a["w_exp_up"].reshape(-1, D, F), a["w_exp_down"].reshape(-1, F, D),
        params, _np.concatenate(list(constants().values()), 1),
        _np.concatenate([a["b_pw2"], a["norm_final"].reshape(1, D)], 0)]
    nc = _bacc.Bacc("TRN2", target_bir_lowering=False, num_devices=1)
    given, args = {}, []
    for i, v in enumerate(arrays):
        v = _np.ascontiguousarray(v)
        given[f"in_{i}"] = v
        args.append(nc.dram_tensor(f"in_{i}", v.shape, _mybir.dt.from_np(v.dtype), kind="ExternalInput").ap())
    for i, shape in enumerate(_VIEWS):
        args.append(nc.dram_tensor(f"out_{i}", shape, _mybir.dt.float32, kind="ExternalOutput").ap())
    build(nc, *args)
    r = _run(nc, [given], core_ids=[0])
    return tuple(r.results[0][f"out_{i}"].reshape(s) for i, s in enumerate(_OUTS))
```

```python
import math
from contextlib import ExitStack

import numpy as np
import concourse.bass as bass
from concourse import mybir

P = 128
D = 1024
KC = D // P
TP, TS = 512, 64
T = TP + TS
NT = 5
NB, NQ = 8, 8
PAST, PAGE = 2048, 128
NPG = PAST // PAGE
HD = 64
HA = 4
NEG = -1e30
EPS = 1e-6
SCALE = HD ** -0.5
LAM_INIT = 0.8 - 0.6 * math.exp(-0.3 * 0)
PATTERNS = ((128, 1), (512, 4), (2048, 16))
NE, F = 32, 512
HB = 64
NX = 20
NPB, NXP = NE // 2, NX // 2
CK = 31
NWIN = 1280
UE = CK - 1 + TP + NB * (CK - 1 + NQ)
FAR = 4.0e6
HALF = T // 2


def rows(t):
    return P if t < 4 else TS


def log_count(dist):
    dist = np.asarray(dist)
    n = sum(((dist >= 0) & (dist % d == 0) & (dist <= w)).astype(np.float32) for w, d in PATTERNS)
    return np.where(n > 0, np.log(np.maximum(n, 1)), NEG).astype(np.float32)


def constants():
    f = np.float32
    c = {}
    r, k = np.arange(P)[:, None], np.arange(P)[None, :]
    c["ident"] = np.eye(P, dtype=f)
    c["ones"] = np.ones((P, P), f)
    c["before"] = (r < k).astype(f)
    c["causal"] = np.where(k <= r, 0, NEG).astype(f)
    c["dilated"] = np.concatenate([log_count(P * d + r - k) for d in (3, 2, 1, 0)], 1)
    q = r % 8
    kk = np.arange(120)[None, :]
    off = kk - 56
    inside = (off >= 0) & (off < 8)
    c["new_diff"] = np.where(inside & (off <= q), 0, NEG).astype(f)
    c["new_win"] = np.where(inside, log_count(np.where(inside, q - off, 0)), NEG).astype(f)
    j = np.arange(NWIN)
    pos = np.where(j < 768, 16 * (j // 8) + j % 8, 1536 + j - 768)
    c["old_win"] = log_count(PAST + q - pos[None, :])
    pair = np.zeros((P, 32), f)
    for h in range(HA):
        for s in range(2):
            for i in range(8):
                pair[32 * h + 8 * s + i, 8 * h + i] = 1
    c["pair"] = pair
    inv = (f(500000.0) ** (-np.arange(8, dtype=f) / f(8))).astype(f)
    rope = np.zeros((P, NT, 2, 8), f)
    for t in range(NT):
        p = (t * P + np.arange(P)) if t < 4 else PAST + np.arange(P) % 8
        ang = (p.astype(f)[:, None] * inv[None, :]).astype(f)
        rope[:, t, 0], rope[:, t, 1] = np.cos(ang), np.sin(ang)
    c["rope"] = rope.reshape(P, -1)
    sub = (np.arange(P) % 32) // 8
    c["coef_one"] = (sub != 1).astype(f)[:, None]
    c["coef_lam"] = -(sub == 1).astype(f)[:, None]
    e = np.arange(NE, dtype=f)
    c["expert_rank"] = np.broadcast_to(NE - e, (P, NE)).astype(f)
    c["expert_base"] = np.broadcast_to(HB * e, (P, NE)).astype(f)
    c["expert_shift"] = np.broadcast_to(HB * (NE - 1 - e), (P, NE)).astype(f)
    c["group_rank"] = np.broadcast_to(4 - np.arange(4, dtype=f), (P, 4)).astype(f)
    code = np.zeros((P, 2, NT, 2), f)
    for t in range(NT):
        for s in range(2):
            code[:, s, t, 0] = t * P + np.arange(P)
            code[:, s, t, 1] = 2 * (t * P + np.arange(P)) + s
    c["codes"] = code.reshape(P, -1)
    valid = np.ones((P, NT), f)
    valid[TS:, 4] = 0
    c["valid"] = valid
    c["extra_no"] = np.broadcast_to(np.arange(NX, dtype=f), (P, NX)).astype(f)
    c["extra_pair"] = np.broadcast_to(2 * np.arange(NXP, dtype=f), (P, NXP)).astype(f)
    return c


PARAMS = [("gain", 32), ("subln", 1), ("w_dw", KC * CK), ("b_dw", KC), ("ln_g", KC), ("ln_b", KC),
          ("b_pw1", 16), ("router", 2 * KC * 36), ("lambdas", 4)]


def build(nc, x_prompt, x_sample, ck, cv, wk, wv, st_rows, st_cols, ptab, w_in, w_out, w_pw1, w_pw2,
          w_g, w_u, w_d, params, consts, vecs,
          y_p, y_s, nkd_p, nvd_p, nkd_s, nvd_s, nwk_p, nwv_p, nwk_s, nwv_s, ncv_p, ncv_s):
    f32, i32 = mybir.dt.float32, mybir.dt.int32
    ALU, ACT, AX = mybir.AluOpType, mybir.ActivationFunctionType, mybir.AxisListType
    ctx = ExitStack()

    def sb(name, shape, dt=f32):
        return ctx.enter_context(nc.sbuf_tensor(name, shape, dt))

    def sem(name):
        return ctx.enter_context(nc.semaphore(name))

    def scratch(name, shape):
        return nc.dram_tensor(name, shape, f32).ap()

    h_rows = [scratch(f"h_rows{l}", (T, D)) for l in range(2)]
    y_rows = [scratch(f"y_rows{l}", (2 * T, D)) for l in range(2)]
    table = [scratch(f"table{l}", ((NPB + NXP) * P, 2)) for l in range(2)]

    ring = sb("ring", [P, 6, 4096])
    x = sb("x", [P, NT * D])
    act_t = sb("act_t", [P, KC, T])
    big = sb("big", [P, 14848])
    cst_np = constants()
    ccol, o = {}, 0
    for name, a in cst_np.items():
        ccol[name] = (o, a.shape[1])
        o += a.shape[1]
    cst = sb("cst", [P, o])
    pcol, o = {}, 0
    for name, w in PARAMS:
        pcol[name] = (o, w)
        o += w
    par = sb("par", [P, o])
    st = sb("st", [P, 112])
    sti = sb("sti", [P, NB * NPG], i32)
    pt_sb = sti[0:1, :]

    def C(name):
        a, w = ccol[name]
        return cst[:, a:a + w]

    def PR(name):
        a, w = pcol[name]
        return par[:, a:a + w]

    xt = x[:, :].rearrange("p (t d) -> p t d", t=NT)
    ident, ones = C("ident"), C("ones")
    gain = PR("gain").rearrange("p (u k) -> p u k", u=4)
    router = PR("router").rearrange("p (l k e) -> p l k e", l=2, k=KC)
    rope = C("rope").rearrange("p (t s d) -> p t s d", t=NT, s=2)
    codes = C("codes").rearrange("p (s t c) -> p s t c", s=2, t=NT)

    def B(a, n, *shape):
        v = big[:, a:a + n]
        if len(shape) == 2:
            v = v.rearrange("p (a b) -> p a b", a=shape[0])
        elif len(shape) == 3:
            v = v.rearrange("p (a b c) -> p a b c", a=shape[0], b=shape[1])
        return v

    def X(a, n, *shape):
        v = x[:, a:a + n]
        if len(shape) == 2:
            v = v.rearrange("p (a b) -> p a b", a=shape[0])
        elif len(shape) == 3:
            v = v.rearrange("p (a b c) -> p a b c", a=shape[0], b=shape[1])
        return v

    qT = [B(0, 2048, 4, 512), B(6144, 2048, 4, 512)]
    kT = [B(2048, 2048, 4, 512), B(8192, 2048, 4, 512)]
    vP = [B(4096, 2048, 4, 512), B(10240, 2048, 4, 512)]
    qS = [B(12288, 576, 9, 4, 16), B(12800, 576, 9, 4, 16)]
    kS = [B(13312, 256, 4, 64), B(13568, 256, 4, 64)]
    vS = [B(13824, 512), B(14336, 512)]
    zrow = X(0, 2048, 4, 512)
    PTsb = X(0, 2048, 2, 2, 512)
    Ex = X(2048, 2048, 2, 2, 512)
    orow = X(4096, 256, 2, 128)
    orow4 = X(4352, 512, 4, 128)
    rtmp = X(4352, 256, 4, 8, 8)
    S_d, S_w = B(0, 2112), B(2112, 1344)
    KTs = B(3456, 4096, 8, 512)
    PT_d, PT_w = B(7552, 2176, 17, 128), B(9728, 1408, 11, 128)
    aux = X(0, 2048, 4, 512)
    O_all = [X(2048, 1024, 8, 128), X(3072, 1024, 8, 128)]
    Qcur = X(4096, 256, 2, 4, 32)
    comb, csq = B(0, 1024, 8, 128), B(1024, 1024, 8, 128)
    xn = B(11776, 2048, 2, D)
    Xg, XgT = B(0, 2048, 2, D), B(2048, 2048, 2, KC, P)
    sg, hb, hbT = B(4096, 512), B(4608, 512), B(5120, 512, 4, P)
    Y = B(5632, 2048, 2, D)
    y01 = B(7680, 4096, 2, 2, D)
    u_ext = B(0, KC * UE, KC, UE)
    cc = B(KC * UE, KC * T, KC, T)
    sig = B(11376, 2 * T, 2, T)
    mr = B(12528, 2 * T, 2, T)
    brow = big[0:1, 13680:13680 + D]
    crow_p, crow_s = B(12528, D)[0:CK - 1], B(12528 + D, D)[0:TS]
    osq = X(4864, 128)
    gf = B(0, D)

    ps = ctx.enter_context(nc.psum_tensor("ps", [P, 8, 512], f32))

    waited = sem("waited")
    stage = {n: sem(f"stage_{n}") for n in ("pe", "act", "dve", "pool")}
    act_step, dve_step, pool_step = sem("act_step"), sem("dve_step"), sem("pool_step")
    loaded = [sem(f"loaded{s}") for s in range(6)]
    consts_in, table_io = sem("consts_in"), sem("table_io")
    rows_out2 = [sem(f"rows_out_{i}") for i in range(2)]
    out_done, copy_done = sem("out_done"), sem("copy_done")
    norm_sq, norm_rows, norm_tr, norm_ev = sem("norm_sq"), sem("norm_rows"), sem("norm_tr"), sem("norm_ev")
    z_mm, z_copy, z_rope, z_tr, z_tev = sem("z_mm"), sem("z_copy"), sem("z_rope"), sem("z_tr"), sem("z_tev")
    z_out = [sem(f"z_out{i}") for i in range(4)]
    a_s, a_max, a_exp, a_p, a_t, a_ptev = sem("a_s"), sem("a_max"), sem("a_exp"), sem("a_p"), sem("a_t"), sem("a_ptev")
    r_slot, a_norm = sem("r_slot"), sem("a_norm")
    a_o, a_sq, a_row, a_ot, a_cat = sem("a_o"), sem("a_sq"), sem("a_row"), sem("a_ot"), sem("a_cat")
    q_ready, t_done, te_act, te_dve, s_mm = sem("q_ready"), sem("t_done"), sem("te_act"), sem("te_dve"), sem("s_mm")
    sd_ev, sw_ev, max_ready, exp_done = sem("sd_ev"), sem("sw_ev"), sem("max_ready"), sem("exp_done")
    pt_done, ptev_act, ptev_dve, pv_done, o_ev = sem("pt_done"), sem("ptev_act"), sem("ptev_dve"), sem("pv_done"), sem("o_ev")
    aux_in = [sem("auxk_in"), sem("auxv_in")]
    f_mm, f_ev, x_first, x_in = sem("f_mm"), sem("f_ev"), sem("x_first"), sem("x_in")
    p_mm, p_ev = sem("p_mm"), sem("p_ev")
    r_mm, r_ev, r_exp = sem("r_mm"), sem("r_ev"), sem("r_exp")
    lam_mm, lam_exp, lam_ready, zeroed = sem("lam_mm"), sem("lam_exp"), sem("lam_ready"), sem("zeroed")
    moe = []
    for l in range(2):
        for kind in ("m", "x"):
            m = {n: sem(f"{kind}{l}_{n}") for n in (
                "gathered0", "gathered1", "xt", "xgt", "g", "silu", "u", "hb", "ht", "hbt", "y", "yev",
                "scattered0", "scattered1") if (kind, n) != ("x", "scattered1")}
            moe.append(m)
    x_loaded = [[sem(f"x_loaded{l}_{kind}") for kind in ("g", "u", "d")] for l in range(2)]
    y_back = [sem("y_back0"), sem("y_back1")]
    y_used, tok_ready, code_ready = sem("y_used"), sem("tok_ready"), sem("code_ready")
    x_tok = [sem("x_tok0"), sem("x_tok1")]
    x_stored = [sem("x_stored0"), sem("x_stored1")]
    pw_mm, pw_sig, glu, state_in = sem("pw_mm"), sem("pw_sig"), sem("glu"), sem("state_in")
    cv_new, ln_sums, ln_squares, ln_steps = sem("cv_new"), sem("ln_sums"), sem("ln_squares"), sem("ln_steps")
    cv_ev, diagonals = sem("cv_ev"), sem("diagonals")

    class Steps:
        def __init__(self, eng, s):
            self.eng, self.s, self.base, self.k = eng, s, 0, 0

        @property
        def n(self):
            return self.base + self.k

        def start(self, base):
            self.base, self.k = base, 0

        def __call__(self, ins):
            ins.then_inc(self.s, 1)
            self.k += 1
            return ins

        def done(self):
            self.eng.wait_ge(self.s, self.n)


    NAMES = ("pe", "act", "dve", "pool")

    class Fence:
        def __init__(self, eng, name):
            self.eng, self.name, self.n = eng, name, 0

        def __call__(self):
            self.n += 1
            self.eng.drain().then_inc(stage[self.name], 1)
            for o in NAMES:
                self.eng.wait_ge(stage[o], self.n)

    with_lead = [s_mm, pv_done, te_act, te_dve, sw_ev, o_ev, ptev_act, ptev_dve]
    with_lead += x_stored
    with_lead += [m[n] for m in moe for n in ("xgt", "g", "silu", "u", "hb", "ht", "hbt", "y", "yev")]

    PER_BATCH = [128, 128, 128, 128, 112, 112]
    AFTER_BATCH = [16 + NB * n for n in PER_BATCH]

    def slot(s, a):
        return ring[:, s, :].rearrange("p (a n) -> p a n", a=a)

    def eslots(par):
        return (2, 3, 4) if par == 0 else (5, 0, 1)

    def moe_base(l, s):
        return AFTER_BATCH[s] + (16 if s < 2 else 0) + l * (16 * 16 + 16)

    qtab = {0: 0, 1: 1, 3: 2, 4: 3}

    def stores_before(k):
        return sum(1 for i in range(k % 4, k, 4) if i // NT in (1, 3) and i < 4 * NT)

    GROUPS = [None, (0, 0, 4, 0), (0, 4, 4, 512), (1, 0, 4, 1024), (1, 4, 4, 1536),
              (4, 0, 4, 0), (4, 4, 4, 512), (None, 0, 2, 1024)]
    CHUNKS = [(0, range(0, 4)), (0, range(4, 8)), (0, range(8, 12)), (0, range(12, 16)), (0, range(16, 17)),
              (1, range(0, 4)), (1, range(4, 8)), (1, range(8, 11))]
    ITEMS = [(qt, kind, c) for qt in range(4) for c in range(4) for kind in (0, 1)]
    NI = len(ITEMS)

    def turned_before(m):
        return sum(1 + (ITEMS[i][2] == 3) for i in range(m) if ITEMS[i][1] == 1)



    SC = 7680
    rcol = {"n": SC}

    def R(*shape):
        n = int(np.prod(shape))
        a = rcol["n"]
        rcol["n"] += n
        return B(a, n, *shape) if len(shape) > 1 else B(a, n)

    L = R(NT, 36)
    g_max, g_sub, g_exp, g_hit, g_top = R(NT), R(NT, 4), R(NT, 4), R(NT, 4), R(NT)
    g_one, g_pen, g_sum, e_all = R(NT, 4), R(NT, 4), R(NT), R(NT, NE)
    m_1, m_2, top, hit = R(NT), R(NT), R(NT), R(NT, NE)
    one = [R(NT, NE), R(NT, NE)]
    e_dif, e_exp, both = R(NT), R(NT), R(NT, NE)
    rank, slot_f, pick = R(NT, NE), R(NT, NE), R(NT, NE)
    count, more, pre_a, pre_b, shift_f = R(NE), R(NE), R(NE), R(NE), R(NE)
    slots, x_hit, x_exp, x_pair = R(2, NT), R(NX, NE), R(NX), R(NXP)
    assert rcol["n"] <= SC + 2560
    tab = B(SC + 2560, 256, P, 2)[0:NPB + NXP]
    wts = st[:, 100:110].rearrange("p (s t) -> p s t", s=2)
    NTB = NPB + NXP
    tokI, codeI = sti[:, 0:NTB], sti[:, NTB:2 * NTB]
    tokS, codeS, slotI = sti[:, 52:54], sti[:, 54:56], sti[:, 100:110]
    XE, XN = 56, 56 + NX

    wdw = PR("w_dw").rearrange("p (c j) -> p c j", c=KC)
    us = u_ext[:, :, CK - 1 + TP:].rearrange("p c (b w) -> p c b w", b=NB)
    PE_CH = (KC - 2, KC - 1)

    block = ctx.enter_context(nc.Block())

    @block.sync
    def _(sp):
        sp.dma_start(xt[:, 0:4, :], x_prompt.rearrange("(t p) d -> p t d", p=P)).then_inc(x_first, 16)
        sp.dma_start(xt[0:TS, 4, :], x_sample).then_inc(x_first, 16)
        sp.dma_start(cst[:, :], consts).then_inc(consts_in, 16)
        sp.dma_start(par[:, :], params).then_inc(consts_in, 16)
        sp.dma_start(pt_sb, ptab).then_inc(consts_in, 16)
        wi = w_in.rearrange("(k p) (n c) -> n p k c", p=P, n=6)
        for n in range(6):
            sp.dma_start(slot(n, 8), wi[n]).then_inc(loaded[n], 16)
        n = PAST - NQ
        for i in range(2 * NB):
            if i < 10:
                sp.wait_ge(z_mm, 4 + 2 * i)
            else:
                sp.wait_ge(a_s, 2 * (i - 10) + 1)
            dst, src = ((nwk_s, wk), (nwv_s, wv))[i % 2]
            sp.dma_start(dst[i // 2, 0:n].rearrange("a c -> (a c)").rearrange("(k n) -> k n", k=16),
                         src[i // 2, NQ:PAST].rearrange("a c -> (a c)").rearrange("(k n) -> k n", k=16)
                         ).then_inc(copy_done, 16)
        sp.dma_start(ncv_s[:, 0:CK - 1 - NQ, :], st_rows[:, NQ:, :]).then_inc(copy_done, 16)
        sp.wait_ge(consts_in, 48)

        def request(b, s_free):
            pages = [sp.value_load(pt_sb[0:1, bass.ds(b * NPG + i, 1)], min_val=0, max_val=ck.shape[0] - 1)
                     for i in range(NPG)]
            for half in range(2):
                s_free(half)
                for i in range(8):
                    sp.dma_start(slot(half, 8)[:, i, :],
                                 ck[bass.ds(pages[8 * half + i], 1)].rearrange("a p c -> (a p) c")
                                 ).then_inc(loaded[half], 16)
            for src, s, a in ((wk, 4, 0), (wv, 5, 1)):
                if a == 0:
                    s_free(4)
                    s_free(6)
                else:
                    for half in range(2):
                        s_free(2 + half)
                        for i in range(8):
                            sp.dma_start(slot(2 + half, 8)[:, i, :],
                                         cv[bass.ds(pages[8 * half + i], 1)].rearrange("a p c -> (a p) c")
                                         ).then_inc(loaded[2 + half], 16)
                    s_free(5)
                    s_free(7)
                one = src[bass.ds(b, 1)].rearrange("a r c -> (a r) c")
                far = one[0:1536].rearrange("(t g r) c -> t g r c", t=6, r=16)[:, :, 0:8]
                for i in range(6):
                    sp.dma_start(slot(s, 8)[:, i, :], far[i]).then_inc(loaded[s], 16)
                recent = one[1536:2048].rearrange("(t p) c -> p t c", p=P)
                sp.dma_start(slot(s, 8)[:, 6:8, :], recent[:, 0:2]).then_inc(loaded[s], 16)
                sp.dma_start(aux[:, 2 * a:2 * a + 2, :], recent[:, 2:4]).then_inc(aux_in[a], 16)

        def first_free(i):
            if i < 6:
                sp.wait_ge(z_mm, 5 * (i + 1))
            else:
                sp.wait_ge(stage["dve"], 3)
                sp.wait_ge(stage["pe"], 3)
                sp.wait_ge(stage["act"], 3)
                sp.wait_ge(stage["pool"], 3)
        request(0, first_free)
        with sp.Fori(1, NB) as b:
            def later_free(i):
                if i in (0, 1, 4, 6):
                    sp.wait_ge(t_done, (b - 1) * 28 + {0: 8, 1: 16, 4: 24, 6: 28}[i])
                    sp.sem_inc(waited)
                else:
                    sp.wait_ge(pv_done, (b - 1) * 8 + {2: 2, 3: 4, 5: 7, 7: 8}[i] + 1)
                    sp.sem_inc(waited)
            request(b, later_free)

        wo = w_out.rearrange("(k p) (n c) -> n p k c", p=P, n=2)
        for n in range(2):
            sp.wait_ge(t_done, (NB - 1) * 28 + 8 * (n + 1))
            sp.dma_start(slot(n, 8), wo[n]).then_inc(loaded[n], 16)

        def expert_load(l, e, par, kind, done):
            t = eslots(par)[kind]
            src = (w_g, w_u, w_d)[kind][bass.ds(e + NE * l, 1)].rearrange("a r c -> (a r) c")
            src = src.rearrange("(k p) c -> p k c", p=P)
            sp.dma_start(slot(t, 8 if kind < 2 else 4), src).then_inc(loaded[t] if done is None else done, 16)

        def moe_weights(l):
            m, mx = moe[2 * l], moe[2 * l + 1]
            for kind in range(3):
                for par_ in range(2):
                    s = eslots(par_)[kind]
                    if l == 0:
                        if s < 2:
                            sp.wait_ge(p_mm, NT * (s + 1))
                        elif s in (2, 3):
                            sp.wait_ge(pv_done, (NB - 1) * 8 + (2, 4)[s - 2] + 1)
                        elif s == 4:
                            sp.wait_ge(t_done, (NB - 1) * 28 + 24)
                        else:
                            sp.wait_ge(pv_done, (NB - 1) * 8 + 8)
                    else:
                        if s < 2:
                            sp.wait_ge(p_mm, 2 * NT + NT * (s + 1))
                        else:
                            sp.wait_ge(pw_mm, (KC + 1, KC + 3)[s - 2] if s < 4 else KC)
                    expert_load(l, par_, par_, kind, None)
            with sp.Fori(1, NPB) as j:
                for kind in range(3):
                    if kind < 2:
                        sp.wait_ge(m["gu"[kind]], j + 1)
                        sp.sem_inc(waited)
                    else:
                        sp.wait_ge(m["y"], 2 * j + 1)
                        sp.sem_inc(waited)
                    for par_ in range(2):
                        expert_load(l, 2 * j + par_, par_, kind, None)
            sp.wait_ge(r_slot, 2 * l + 2)
            n_pairs = sp.value_load(sti[0:1, XN:XN + 1], min_val=0, max_val=NXP)
            with sp.Fori(0, NXP) as j:
                with sp.If(n_pairs > j):
                    for kind in range(3):
                        if kind < 2:
                            sp.wait_ge(m["gu"[kind]], NPB + 1)
                            sp.wait_ge(mx["gu"[kind]], j + 1)
                            sp.sem_inc(waited)
                        else:
                            sp.wait_ge(m["y"], 2 * NPB + 1)
                            sp.wait_ge(mx["y"], 2 * j + 1)
                            sp.sem_inc(waited)
                        for par_ in range(2):
                            e = sp.value_load(sti[0:1, bass.ds(2 * j + XE + par_, 1)], min_val=0, max_val=NE - 1)
                            expert_load(l, e, par_, kind, x_loaded[l][kind])

        moe_weights(0)
        w1 = w_pw1.rearrange("(k p) (n c) -> n p k c", p=P, n=4)
        sp.wait_ge(stage["pe"], 10)
        sp.wait_ge(y_back[1], 32)
        for s, n in ((2, 0), (3, 2), (4, 1), (5, 3)):
            sp.dma_start(slot(s, 8), w1[n]).then_inc(loaded[s], 16)
        w2 = w_pw2.rearrange("(k p) (n c) -> n p k c", p=P, n=2)
        sp.wait_ge(pw_mm, 1)
        for n in range(2):
            sp.dma_start(slot(n, 8), w2[n]).then_inc(loaded[n], 16)
        moe_weights(1)
        sp.wait_ge(copy_done, 2 * NB * 16 + 16)

    @block.scalar
    def _(act):
        A = Steps(act, act_step)
        fence = Fence(act, "act")
        A_ = nc.scalar.activation

        def copy(o, i):
            return A_(o, i, ACT.Copy)

        def norm(u):
            for t in range(NT):
                r = rows(t)
                if u in (1, 3):
                    act.wait_ge(p_ev, (u // 2) * 2 * NT + NT + t + 1)
                if u in (2, 4):
                    act.wait_ge(y_used, (u // 2 - 1) * NT + t + 1)
                if t:
                    A.done()
                A(A_(xn[0:r, 0, :], xt[0:r, t, :], ACT.Square, accum_out=st[0:r, t:t + 1]))
            A.done()
            act.drain().then_inc(norm_sq, 1)

        act.wait_ge(lam_mm, 1)
        A_(st[:, 20:22], ps[:, 7, 0:2], ACT.Exp).then_inc(lam_exp, 1)
        act.wait_ge(x_first, 32)
        act.wait_ge(zeroed, 1)
        norm(0)
        fence()

        i_z = 0
        for n in range(6):
            for t in range(NT):
                r = rows(t)
                act.wait_ge(z_mm, i_z + 1)
                bank = ps[0:r, 4 + i_z % 4, :]
                i_z += 1
                if n in qtab:
                    k = qtab[n] * NT + t
                    if k > 3:
                        act.wait_ge(z_tr, k - 3)
                    if 16 * stores_before(k) > 0:
                        act.wait_ge(z_out[k % 4], 16 * stores_before(k))
                    if n < 2:
                        copy(zrow[0:r, k % 4, :].rearrange("p (h s d) -> p s h d", h=4, s=2),
                             bank.rearrange("p (s h d) -> p s h d", h=4, s=2)).then_inc(z_copy, 1)
                    else:
                        copy(zrow[0:r, k % 4, :], bank).then_inc(z_copy, 1)
                else:
                    dst = vP[n // 4][:, t, :] if t < 4 else vS[n // 4][0:r, :]
                    copy(dst, bank).then_inc(z_copy, 1)
        fence()

        for s in range(NI + 3):
            if s < NI:
                qt, kind, c = ITEMS[s]
                n = (qt + 1) * P
                act.wait_ge(a_max, s + 1)
                if s > 1:
                    act.wait_ge(a_t, s - 1)
                if s > 1:
                    act.wait_ge(a_p, s - 1)
                for j in range(2):
                    a = 2 * (s % 2) + j
                    A_(Ex[:, s % 2, j, 0:n], ps[:, a, 0:n], ACT.Exp, bias=st[:, 32 + a:33 + a],
                       scale=(SCALE if kind == 0 else 1.0), accum_out=st[:, 36 + a:37 + a]).then_inc(a_exp, 1)
            m = s - 1
            if 0 <= m < NI:
                qt, kind, c = ITEMS[m]
                n = (qt + 1) * P
                act.wait_ge(a_t, m + 1)
                if m > 1:
                    act.wait_ge(a_o, m - 1)
                if kind == 0:
                    copy(PTsb[:, m % 2, 0, 0:n], ps[:, 4, 0:n]).then_inc(a_ptev, 1)
                else:
                    copy(PTsb[:, m % 2, :, 0:n], ps[:, 4:6, 0:n]).then_inc(a_ptev, 1)
            m = s - 2
            if 0 <= m < NI and ITEMS[m][1] == 0:
                qt, kind, c = ITEMS[m]
                act.wait_ge(a_row, m + 1)
                if qt > 0:
                    act.wait_ge(a_norm, qt)
                if A.k:
                    A.done()
                A(A_(osq, orow4[:, c, :], ACT.Square, accum_out=st[:, 44 + c:45 + c]))
                if c == 3:
                    A.done()
                    act.drain().then_inc(a_sq, 1)
        fence()
        fence()

        with act.Fori(0, NB) as b:
            def tev(g):
                nb = GROUPS[g][2]
                for c in (0, 2):
                    act.wait_ge(t_done, b * 28 + 4 * (g - 1) + c + 1)
                    act.wait_ge(s_mm, (b * 8 + (0 if g <= 2 else g - 1)) + 1)
                    copy(KTs[:, 4 * (g % 2) + c, 0:nb * P], ps[:, 0, 0:nb * P]).then_inc(te_act, 1)

            def sd(g):
                act.wait_ge(s_mm, b * 8 + g + 2)
                act.wait_ge(pv_done, b * 8 + 1)
                copy(S_d[:, (g - 1) * 512:g * 512], ps[:, 2 + g % 2, :]).then_inc(sd_ev, 1)

            tev(1); tev(2); sd(1); tev(3); sd(2); tev(4); sd(3); tev(5); sd(4); tev(6)
            act.wait_ge(max_ready, b * 2 + 1)
            A_(S_d, S_d, ACT.Exp, bias=st[:, 48:49], scale=SCALE, accum_out=st[:, 50:51]).then_inc(exp_done, 1)
            tev(7)
            act.wait_ge(max_ready, b * 2 + 2)
            A_(S_w, S_w, ACT.Exp, bias=st[:, 49:50], scale=1.0, accum_out=st[:, 51:52]).then_inc(exp_done, 1)
            for k in (1, 3, 5):
                w, blocks = CHUNKS[k]
                act.wait_ge(pt_done, b * 8 + k + 1)
                copy((PT_w if w else PT_d)[:, blocks[0]:blocks[-1] + 1, :],
                     ps[:, 5, :].rearrange("p (n c) -> p n c", c=P)).then_inc(ptev_act, 1)
            act.wait_ge(pt_done, b * 8 + 8)
            copy(PT_w[:, 8:10, :], ps[:, 5, 0:256].rearrange("p (n c) -> p n c", c=P)).then_inc(ptev_act, 1)
            copy(PT_w[0:TS, 10, :], ps[0:TS, 5, 256:384]).then_inc(ptev_act, 1)
        fence()
        act.wait_ge(f_mm, 1)
        copy(comb[0:32, :, :].rearrange("p b d -> p (b d)"),
             ps[0:32, 0:2, :].rearrange("p a n -> p (a n)")).then_inc(f_ev, 1)
        fence()
        norm(1)
        fence()

        def silu_step(m, n):
            act.wait_ge(m["g"], n + 2)
            act.wait_ge(m["hb"], n + 1)
            A_(sg, ps[:, 0, :], ACT.Silu).then_inc(m["silu"], 1)

        def hbt_step(m, n):
            act.wait_ge(m["ht"], n + 2)
            act.wait_ge(m["y"], 2 * n + 1)
            copy(hbT, ps[:, 4, :].rearrange("p (k c) -> p k c", k=4)).then_inc(m["hbt"], 1)

        def y_step(m, n, par_, used):
            for h in range(2):
                act.wait_ge(m["y"], 2 * n + h + 2)
                if used is not None and h == 0:
                    act.wait_ge(m[f"scattered{par_}"], used)
                copy(Y[:, par_, h * 512:(h + 1) * 512], ps[:, 5 + h, :]).then_inc(m["yev"], 1)

        def layer_ffn(l):
            fence()
            act.wait_ge(r_ev, 3 * l + 1)
            A_(g_exp, g_sub, ACT.Exp).then_inc(r_exp, 1)
            act.wait_ge(r_ev, 3 * l + 2)
            A_(e_exp, e_dif, ACT.Exp).then_inc(r_exp, 1)
            fence()
            m, mx = moe[2 * l], moe[2 * l + 1]
            for n in range(2):
                silu_step(m, n); hbt_step(m, n); y_step(m, n, n, None)
            with act.Fori(1, NPB // 2) as j:
                silu_step(m, 2 * j); hbt_step(m, 2 * j); y_step(m, 2 * j, 0, j * 16)
                silu_step(m, 2 * j + 1); hbt_step(m, 2 * j + 1); y_step(m, 2 * j + 1, 1, j * 16)
            n_pairs = act.value_load(sti[0:1, XN:XN + 1], min_val=0, max_val=NXP)
            act.wait_ge(m["scattered0"], 16 * NPB // 2)
            with act.Fori(0, NXP) as j:
                with act.If(n_pairs > j):
                    silu_step(mx, j); hbt_step(mx, j)
                    act.wait_ge(x_stored[l], 2 * j + 1)
                    act.sem_inc(waited)
                    y_step(mx, j, 0, None)
            norm(2 + 2 * l)
            fence()

        layer_ffn(0)
        fence()
        for ch in range(KC):
            act.wait_ge(pw_mm, ch + 1)
            if ch > 1:
                act.wait_ge(glu, ch - 1)
            bank = 4 * (ch % 2)
            A_(sig[:, ch % 2, :].rearrange("p (h n) -> p h n", h=2), ps[:, bank + 2:bank + 4, 0:HALF],
               ACT.Sigmoid, bias=PR("b_pw1")[:, 8 + ch:9 + ch], scale=1.0).then_inc(pw_sig, 1)
            if ch in (4, 5):
                c = PE_CH[ch - 4]
                for j in range(CK):
                    ins = A_(slot(ch - 2, 32)[:, j, :], ident, ACT.Copy, scale=wdw[:, c, j:j + 1])
                ins.then_inc(diagonals, 1)
        act.wait_ge(glu, KC)
        copy(act_t[:, :, 0:TS].rearrange("p c (b q) -> p c b q", b=NB),
             u_ext[:, :, CK - 1 + TP:].rearrange("p c (b w) -> p c b w", b=NB)[:, :, :, CK - 1:]).then_inc(cv_new, 1)

        def tap_sums(i):
            c = PE_CH[i]
            A_(cc[:, c, 0:TP], ps[:, 2 * i, :], ACT.Identity, bias=PR("b_dw")[:, c:c + 1], scale=1.0)
            A_(cc[:, c, TP:T], ps[:, 2 * i + 1, 0:TS], ACT.Identity, bias=PR("b_dw")[:, c:c + 1], scale=1.0)

        act.wait_ge(pw_mm, KC + 2)
        copy(crow_p, ps[0:CK - 1, 4:6, :].rearrange("p a n -> p (a n)")).then_inc(cv_ev, 1)
        copy(crow_s, ps[0:TS, 6:8, :].rearrange("p a n -> p (a n)")).then_inc(cv_ev, 1)
        tap_sums(0)
        act.wait_ge(pw_mm, KC + 3)
        tap_sums(1)
        fence()
        act.wait_ge(ln_steps, 1)
        for ch in range(KC):
            if ch > 1:
                act.wait_ge(ln_sums, ch)
            A_(sig[:, ch % 2, :], cc[:, ch, :], ACT.Square).then_inc(ln_squares, 1)
        act.wait_ge(ln_steps, 2)
        A_(mr[:, 1, :], mr[:, 1, :], ACT.Sqrt).then_inc(ln_squares, 1)
        for ch in range(KC):
            act.wait_ge(ln_steps, ch + 3)
            A_(cc[:, ch, :], cc[:, ch, :], ACT.Silu, bias=PR("ln_b")[:, ch:ch + 1],
               scale=PR("ln_g")[:, ch:ch + 1])
        fence()
        norm(3)
        fence()
        layer_ffn(1)

    @block.vector
    def _(dve):
        V = nc.vector
        S = Steps(dve, dve_step)
        fence = Fence(dve, "dve")

        def link(ins):
            S(ins)
            S.done()

        V.memset(st[:, :], 1.0).then_inc(zeroed, 1)
        dve.wait_ge(zeroed, 1)
        dve.wait_ge(consts_in, 48)
        lam4 = PR("lambdas")
        link(V.tensor_tensor(st[:, 22:23], lam4[:, 0:1], lam4[:, 1:2], ALU.mult))
        S(V.tensor_tensor(st[:, 23:24], lam4[:, 2:3], lam4[:, 3:4], ALU.mult))
        S.done()
        dve.drain().then_inc(lam_ready, 1)
        dve.wait_ge(lam_exp, 1)
        link(V.tensor_tensor(st[:, 25:26], st[:, 20:21], st[:, 21:22], ALU.subtract))
        link(V.tensor_scalar(st[:, 25:26], st[:, 25:26], LAM_INIT, None, ALU.add))
        link(V.scalar_tensor_tensor(st[:, 24:25], C("coef_lam"), st[:, 25:26], C("coef_one"), ALU.mult, ALU.add))
        link(V.tensor_scalar(st[:, 25:26], st[:, 25:26], -1.0, None, ALU.mult))

        def rstd(o, i, n):
            p, w = o.shape
            v, half, t = (st[0:p, a:a + w] for a in (70, 78, 86))
            link(V.tensor_scalar(v, i, 1.0 / n, EPS, ALU.mult, ALU.add))
            link(V.tensor_scalar(half, v, -0.5, None, ALU.mult))
            link(V.tensor_scalar(t.bitcast(i32), v.bitcast(i32), 1, None, ALU.arith_shift_right))
            link(V.tensor_scalar(o.bitcast(i32), t.bitcast(i32), -1, 0x5f3759df, ALU.mult, ALU.add))
            for _ in range(3):
                link(V.tensor_tensor(t, o, o, ALU.mult))
                link(V.tensor_tensor(t, t, half, ALU.mult))
                link(V.scalar_tensor_tensor(o, t, 1.5, o, ALU.add, ALU.mult))

        def norm(u):
            dve.wait_ge(norm_sq, u + 1)
            rstd(st[:, 5:10], st[:, 0:5], D)

            def turned(t):
                r = rows(t)
                dve.wait_ge(norm_tr, NT * u + t + 1)
                src = ps[:, 2 * (t % 2):2 * (t % 2) + 2, :].rearrange("p a (k c) -> p (a k) c", k=4)
                V.tensor_tensor(act_t[:, :, t * P:t * P + r], src[:, :, 0:r],
                                gain[:, u, :].unsqueeze(2).broadcast_to((P, KC, r)), ALU.mult).then_inc(norm_ev, 1)

            for t in range(NT):
                r = rows(t)
                if t >= 2:
                    dve.wait_ge(norm_tr, NT * u + t - 1)
                    if u in (1, 3):
                        dve.wait_ge(rows_out2[t % 2], 16 * ((u // 2) * (3 - t % 2) + t // 2))
                V.tensor_scalar(xn[0:r, t % 2, :], xt[0:r, t, :], st[0:r, 5 + t:6 + t], None,
                                ALU.mult).then_inc(norm_rows, 1)
                if t:
                    turned(t - 1)
            turned(NT - 1)

        norm(0)
        fence()

        def z_turned(n, t, k):
            dve.wait_ge(z_tr, k + 1)
            src = ps[:, k % 2, :].rearrange("p (h c) -> p h c", h=4)
            w = n // 3
            if t < 4:
                dst = (kT if n in (1, 4) else qT)[w]
                V.tensor_copy(dst[:, :, t * P:(t + 1) * P], src).then_inc(z_tev, 1)
            elif n in (1, 4):
                V.tensor_copy(kS[w], src[:, :, 0:TS]).then_inc(z_tev, 1)
            else:
                for j in range(2):
                    p = slice(64 * j, 64 * j + 64)
                    for h in range(4):
                        ins = V.tensor_copy(qS[w][p, 0:NB, h, 8 * j:8 * j + 8],
                                            src[p, h, 0:TS].rearrange("p (b q) -> p b q", b=NB))
                        if j == 1 and h == 3:
                            ins.then_inc(z_tev, 1)

        link(V.memset(B(12288, 1024), 0.0))
        prev = None
        i_z = 0
        for n in range(6):
            for t in range(NT):
                i_z += 1
                if n not in qtab:
                    continue
                r, k = rows(t), qtab[n] * NT + t
                dve.wait_ge(z_copy, i_z)
                if k > 0:
                    dve.wait_ge(z_rope, k)
                z3 = zrow[0:r, k % 4, :].rearrange("p (g d) -> p g d", g=8)
                x1, x2 = z3[:, :, 0:8], z3[:, :, 8:16]
                cos = rope[0:r, t, 0:1, :].broadcast_to((r, 8, 8))
                sin = rope[0:r, t, 1:2, :].broadcast_to((r, 8, 8))
                S(V.tensor_tensor(rtmp[0:r, 0], x1, cos, ALU.mult))
                S(V.tensor_tensor(rtmp[0:r, 1], x2, sin, ALU.mult))
                S(V.tensor_tensor(rtmp[0:r, 2], x2, cos, ALU.mult))
                S(V.tensor_tensor(rtmp[0:r, 3], x1, sin, ALU.mult))
                S.done()
                S(V.tensor_tensor(x1, rtmp[0:r, 0], rtmp[0:r, 1], ALU.subtract))
                V.tensor_tensor(x2, rtmp[0:r, 2], rtmp[0:r, 3], ALU.add).then_inc(z_rope, 1)
                if prev:
                    z_turned(*prev)
                prev = (n, t, k)
        z_turned(*prev)
        fence()

        def recip(m):
            return st[:, 54 + 2 * (m % 3):56 + 2 * (m % 3)]

        def out_of_bank(m):
            if 0 <= m < NI:
                qt, kind, c = ITEMS[m]
                dve.wait_ge(a_o, m + 1)
                if kind == 0:
                    if qt > 0:
                        dve.wait_ge(a_ot, turned_before(8 * qt))
                    V.tensor_copy(orow4[:, c, :], ps[:, 6, 0:P]).then_inc(a_row, 1)
                else:
                    if m > 4:
                        dve.wait_ge(a_ot, turned_before(m - 4) + 1)
                    V.tensor_tensor(orow[:, c % 2, :].rearrange("p (j d) -> p j d", j=2),
                                    ps[:, 6, 0:P].rearrange("p (j d) -> p j d", j=2),
                                    recip(m).unsqueeze(2).broadcast_to((P, 2, HD)), ALU.mult).then_inc(a_row, 1)
                if (kind, c) == (1, 3):
                    dve.wait_ge(a_sq, qt + 1)
                    dve.wait_ge(a_row, m)
                    rstd(st[:, 60:64], st[:, 44:48], P)
                    V.tensor_tensor(orow4, orow4, st[:, 60:64].unsqueeze(2).broadcast_to((P, 4, P)),
                                    ALU.mult).then_inc(a_norm, 1)

        def into_cat(m):
            if 0 <= m < NI and ITEMS[m][1] == 1:
                qt, kind, c = ITEMS[m]
                done = turned_before(m)
                q = slice(qt * P, (qt + 1) * P)
                dve.wait_ge(a_ot, done + 1)
                V.tensor_copy(act_t[:, 4 + c, q], ps[:, 7, 0:P]).then_inc(a_cat, 1)
                if c == 3:
                    dve.wait_ge(a_ot, done + 2)
                    V.tensor_scalar(act_t[:, 0:4, q], ps[:, 7, :].rearrange("p (c q) -> p c q", c=4), PR("subln"),
                                    1.0 - LAM_INIT, ALU.mult, ALU.mult).then_inc(a_cat, 1)

        for s in range(NI + 3):
            if s < NI:
                qt, kind, c = ITEMS[s]
                n = (qt + 1) * P
                a = 2 * (s % 2)
                dve.wait_ge(a_s, s + 1)
                if 2 * (s - 1) > 0:
                    dve.wait_ge(a_exp, 2 * (s - 1))
                sc = ps[:, a:a + 2, 0:n]
                if kind == 0:
                    diag = ps[:, a:a + 2, n - P:n]
                    link(V.tensor_tensor(diag, diag, C("causal").unsqueeze(1).broadcast_to((P, 2, P)), ALU.add))
                else:
                    msk = C("dilated")[:, (3 - qt) * P:].unsqueeze(1).broadcast_to((P, 2, n))
                    link(V.scalar_tensor_tensor(sc, sc, SCALE, msk, ALU.mult, ALU.add))
                link(V.tensor_reduce(st[:, 32 + a:34 + a], sc, AX.X, ALU.max))
                V.tensor_scalar(st[:, 32 + a:34 + a], st[:, 32 + a:34 + a], -SCALE if kind == 0 else -1.0, None,
                                ALU.mult).then_inc(a_max, 1)
            if s < NI:
                qt, kind, c = ITEMS[s]
                n = (qt + 1) * P
                a = 2 * (s % 2)
                dve.wait_ge(a_exp, 2 * (s + 1))
                if s > 2:
                    dve.wait_ge(a_row, s - 2)
                rc = recip(s)
                if kind == 0:
                    link(V.reciprocal(rc, st[:, 36 + a:38 + a]))
                    S(V.tensor_scalar(Ex[:, s % 2, 0, 0:n], Ex[:, s % 2, 0, 0:n], rc[:, 0:1], None, ALU.mult))
                    link(V.tensor_tensor(rc[:, 1:2], rc[:, 1:2], st[:, 25:26], ALU.mult))
                    V.scalar_tensor_tensor(Ex[:, s % 2, 0, 0:n], Ex[:, s % 2, 1, 0:n], rc[:, 1:2],
                                           Ex[:, s % 2, 0, 0:n], ALU.mult, ALU.add).then_inc(a_p, 1)
                else:
                    V.reciprocal(rc, st[:, 36 + a:38 + a]).then_inc(a_p, 1)
            if s > 2 and ITEMS[(s - 3) % NI][1:] == (1, 3):
                into_cat(s - 3)
                out_of_bank(s - 2)
            else:
                out_of_bank(s - 2)
                into_cat(s - 3)
        fence()
        S(V.memset(Qcur, 0.0))
        S(V.memset(ps[:, 6:8, 0:P], 0.0))
        S.done()
        for w in range(2):
            ins = V.tensor_copy(Qcur[:, w, :, 0:16], qS[w][:, 0, :, :])
        S(ins)
        S.done()
        dve.drain().then_inc(q_ready, 1)
        fence()

        steps0 = S.n
        PER = 6
        with dve.Fori(0, NB) as b:
            S.start(b * PER + steps0)

            def tev(g):
                nb = GROUPS[g][2]
                for c in (1, 3):
                    dve.wait_ge(t_done, b * 28 + 4 * (g - 1) + c + 1)
                    dve.wait_ge(s_mm, (b * 8 + (0 if g <= 2 else g - 1)) + 1)
                    V.tensor_copy(KTs[:, 4 * (g % 2) + c, 0:nb * P], ps[:, 1, 0:nb * P]).then_inc(te_dve, 1)

            def sw(g):
                dve.wait_ge(s_mm, b * 8 + g + 2)
                dve.wait_ge(pv_done, b * 8 + 1)
                at, n = (g - 5) * 512, GROUPS[g][2] * P
                V.scalar_tensor_tensor(S_w[:, at:at + n], ps[:, 2 + g % 2, 0:n], SCALE,
                                       C("old_win")[:, at:at + n], ALU.mult, ALU.add).then_inc(sw_ev, 1)

            tev(1)
            dve.wait_ge(s_mm, b * 8 + 2)
            dve.sem_inc(waited)
            dve.wait_ge(pv_done, b * 8 + 1)
            dve.sem_inc(waited)
            at = 56 - b * 8
            a0, _ = ccol["new_diff"]
            a1, _ = ccol["new_win"]
            S(V.tensor_tensor(S_d[:, PAST:PAST + TS], ps[:, 2, 0:TS], cst[:, bass.ds(at + a0, TS)], ALU.add))
            V.scalar_tensor_tensor(S_w[:, NWIN:NWIN + TS], ps[:, 2, TS:2 * TS], SCALE,
                                   cst[:, bass.ds(at + a1, TS)], ALU.mult, ALU.add).then_inc(sw_ev, 1)
            tev(2); tev(3); tev(4); tev(5)
            dve.wait_ge(sd_ev, b * 4 + 4)
            S.done()
            link(V.tensor_reduce(st[:, 48:49], S_d, AX.X, ALU.max))
            V.tensor_scalar(st[:, 48:49], st[:, 48:49], -SCALE, None, ALU.mult).then_inc(max_ready, 1)
            tev(6); sw(5); tev(7); sw(6); sw(7)
            dve.wait_ge(sw_ev, b * 4 + 5)
            link(V.tensor_reduce(st[:, 49:50], S_w, AX.X, ALU.max))
            V.tensor_scalar(st[:, 49:50], st[:, 49:50], -1.0, None, ALU.mult).then_inc(max_ready, 1)
            S(V.tensor_copy(Qcur[:, 0, :, 0:16], qS[0][:, bass.ds(b + 1, 1), :, :].rearrange("p a h c -> p (a h) c")))
            V.tensor_copy(Qcur[:, 1, :, 0:16],
                          qS[1][:, bass.ds(b + 1, 1), :, :].rearrange("p a h c -> p (a h) c")).then_inc(q_ready, 1)
            for k in (0, 2, 4, 6):
                w, blocks = CHUNKS[k]
                r = TS if k == 4 else P
                dve.wait_ge(pt_done, b * 8 + k + 1)
                V.tensor_copy((PT_w if w else PT_d)[0:r, blocks[0]:blocks[-1] + 1, :],
                              ps[0:r, 4, 0:len(blocks) * P].rearrange("p (n c) -> p n c", c=P)).then_inc(ptev_dve, 1)
            dve.wait_ge(exp_done, b * 2 + 2)
            link(V.reciprocal(st[:, 52:54], st[:, 50:52]))
            link(V.tensor_tensor(st[:, 52:53], st[:, 52:53], st[:, 24:25], ALU.mult))
            dve.wait_ge(pv_done, b * 8 + 9)
            dve.sem_inc(waited)
            for w in range(2):
                ins = V.tensor_scalar(O_all[w][:, bass.ds(b, 1), :].rearrange("p a d -> p (a d)"), ps[:, 6 + w, 0:P],
                                      st[:, 52 + w:53 + w], None, ALU.mult)
                ins.then_inc(o_ev, 1)
            assert S.k == PER, S.k
        S.start(steps0 + NB * PER)
        fence()
        dve.wait_ge(f_ev, 1)
        c32, q32 = comb[0:32], csq[0:32]
        link(V.tensor_tensor(q32, c32, c32, ALU.mult))
        link(V.tensor_reduce(st[0:32, 54:62], q32, AX.X, ALU.add))
        rstd(st[0:32, 54:62], st[0:32, 54:62], P)
        V.tensor_tensor(c32, c32, st[0:32, 54:62].unsqueeze(2).broadcast_to((32, NB, P)), ALU.mult).then_inc(f_ev, 1)
        dve.wait_ge(f_mm, 2)
        new = act_t[:, :, TP:T].rearrange("p k (b q) -> p k b q", b=NB)
        wide = ps[:, 3:5, :].rearrange("p a (b h c) -> p (a b) h c", b=4, h=4)
        for h in range(4):
            V.tensor_scalar(new[:, h], ps[:, 2, 0:256].rearrange("p (b h q) -> p b h q", b=NB, h=4)[:, :, h, :],
                            PR("subln"), 1.0 - LAM_INIT, ALU.mult, ALU.mult)
            for j in range(2):
                p = slice(64 * j, 64 * j + 64)
                V.tensor_copy(new[p, 4 + h], wide[p, :, h, 8 * j:8 * j + 8])
        fence()

        def residual(u):
            for i in range(2 * NT):
                n, t = divmod(i, NT)
                r = rows(t)
                dve.wait_ge(p_mm, u * 2 * NT + i + 1)
                xx = xt[0:r, t, n * 512:(n + 1) * 512]
                V.tensor_tensor(xx, xx, ps[0:r, i % 4, :], ALU.add).then_inc(p_ev, 1)

        dve.wait_ge(x_in, 32)
        residual(0)
        fence()

        def hb_step(m, n):
            dve.wait_ge(m["u"], n + 2)
            dve.wait_ge(m["silu"], n + 2)
            dve.wait_ge(m["ht"], n + 1)
            V.tensor_tensor(hb, sg, ps[:, 1, :], ALU.mult).then_inc(m["hb"], 1)

        def xgt_step(l, m, n, par_, free):
            dve.wait_ge(m["xt"], n + 1)
            if free is not None:
                dve.wait_ge(m["u"], free + 1)
            V.tensor_tensor(XgT[:, par_], ps[:, 2:4, :].rearrange("p a (k c) -> p (a k) c", k=4),
                            gain[:, 1 + 2 * l, :].unsqueeze(2).broadcast_to((P, KC, P)),
                            ALU.mult).then_inc(m["xgt"], 1)

        def layer_ffn(l):
            norm(1 + 2 * l)
            fence()
            link(V.memset(L, 0.0))
            dve.wait_ge(r_mm, 3 * l + 1)
            S(V.tensor_copy(L[:, 0:4, :], ps[:, 7, 0:144].rearrange("p (t e) -> p t e", t=4)))
            link(V.tensor_copy(L[0:TS, 4, :], ps[0:TS, 7, 144:180]))
            Lg, Le = L[:, :, 0:4], L[:, :, 4:36]

            def wide_(a, n):
                return a.unsqueeze(2).broadcast_to((P, NT, n))

            def first_hit(o, v, m, rank_, n, top_, tmp):
                link(V.tensor_tensor(tmp, v, wide_(m, n), ALU.is_equal))
                link(V.tensor_tensor(tmp, tmp, rank_.unsqueeze(1).broadcast_to((P, NT, n)), ALU.mult))
                link(V.tensor_reduce(top_, tmp, AX.X, ALU.max))
                link(V.tensor_tensor(o, tmp, wide_(top_, n), ALU.is_equal))

            link(V.tensor_reduce(g_max, Lg, AX.X, ALU.max))
            V.tensor_tensor(g_sub, Lg, wide_(g_max, 4), ALU.subtract).then_inc(r_ev, 1)
            first_hit(g_one, Lg, g_max, C("group_rank"), 4, g_top, g_hit)
            link(V.tensor_scalar(g_pen, g_one, 1.0, 1e30, ALU.subtract, ALU.mult))
            e4 = e_all.rearrange("p t (g e) -> p t g e", g=4)
            for g in range(4):
                S(V.tensor_tensor(e4[:, :, g, :], Le[:, :, 8 * g:8 * g + 8],
                                  g_one[:, :, g:g + 1].broadcast_to((P, NT, 8)), ALU.mult))
            S.done()
            for g in range(4):
                S(V.tensor_tensor(e4[:, :, g, :], e4[:, :, g, :],
                                  g_pen[:, :, g:g + 1].broadcast_to((P, NT, 8)), ALU.add))
            S.done()
            link(V.tensor_reduce(m_1, e_all, AX.X, ALU.max))
            first_hit(one[0], e_all, m_1, C("expert_rank"), NE, top, hit)
            link(V.scalar_tensor_tensor(e_all, one[0], -2e30, e_all, ALU.mult, ALU.add))
            link(V.tensor_reduce(m_2, e_all, AX.X, ALU.max))
            V.tensor_tensor(e_dif, m_2, m_1, ALU.subtract).then_inc(r_ev, 1)
            first_hit(one[1], e_all, m_2, C("expert_rank"), NE, top, hit)
            link(V.tensor_tensor(both, one[0], one[1], ALU.add))
            V.tensor_tensor(both, both, wide_(C("valid"), NE), ALU.mult).then_inc(r_ev, 1)
            dve.wait_ge(r_exp, 2 * l + 1)
            link(V.tensor_reduce(g_sum, g_exp, AX.X, ALU.add))
            dve.wait_ge(r_exp, 2 * l + 2)
            link(V.scalar_tensor_tensor(g_sum, e_exp, 1.0, g_sum, ALU.add, ALU.mult))
            link(V.reciprocal(wts[:, 0], g_sum))
            link(V.tensor_tensor(wts[:, 1], wts[:, 0], e_exp, ALU.mult))
            dve.wait_ge(r_mm, 3 * l + 2)
            S(V.tensor_copy(rank, ps[:, 6, 0:160].rearrange("p (t e) -> p t e", t=NT)))
            S(V.tensor_copy(count, ps[:, 6, 160:192]))
            S.done()
            link(V.tensor_scalar(more, count, float(HB), None, ALU.is_gt))
            for i in range(2, T // HB):
                link(V.scalar_tensor_tensor(more, count, float(HB * i), more, ALU.is_gt, ALU.add))
            src, dst = more, pre_a
            for k in (1, 2, 4, 8, 16):
                S(V.tensor_copy(dst[:, 0:k], src[:, 0:k]))
                link(V.tensor_tensor(dst[:, k:NE], src[:, k:NE], src[:, 0:NE - k], ALU.add))
                src, dst = dst, (pre_b if dst is pre_a else pre_a)
            incl = src
            link(V.tensor_tensor(shift_f, incl, more, ALU.subtract))
            link(V.scalar_tensor_tensor(shift_f, shift_f, float(HB), C("expert_shift"), ALU.mult, ALU.add))
            link(V.scalar_tensor_tensor(slot_f, rank, float(HB), shift_f.unsqueeze(1).broadcast_to((P, NT, NE)),
                                        ALU.is_ge, ALU.mult))
            link(V.tensor_tensor(slot_f, slot_f, rank, ALU.add))
            link(V.tensor_tensor(slot_f, slot_f, C("expert_base").unsqueeze(1).broadcast_to((P, NT, NE)), ALU.add))
            for s in range(2):
                link(V.tensor_tensor(pick, slot_f, one[s], ALU.mult))
                link(V.tensor_reduce(slots[:, s], pick, AX.X, ALU.add))
            V.tensor_copy(slotI, slots.rearrange("p s t -> p (s t)")).then_inc(r_slot, 1)
            r0 = slice(0, 1)
            link(V.tensor_tensor(x_hit[r0], incl[r0].unsqueeze(1).broadcast_to((1, NX, NE)),
                                 C("extra_no")[r0].unsqueeze(2).broadcast_to((1, NX, NE)), ALU.is_le))
            link(V.tensor_reduce(x_exp[r0], x_hit[r0], AX.X, ALU.add))
            link(V.tensor_scalar(x_exp[r0], x_exp[r0], float(NE - 1), None, ALU.min))
            link(V.tensor_copy(sti[r0, XE:XE + NX], x_exp[r0]))
            link(V.tensor_tensor(x_pair[r0], C("extra_pair")[r0], incl[r0, NE - 1:NE].broadcast_to((1, NXP)), ALU.is_lt))
            link(V.tensor_reduce(x_exp[r0, 0:1], x_pair[r0], AX.X, ALU.add))
            V.tensor_copy(sti[r0, XN:XN + 1], x_exp[r0, 0:1]).then_inc(r_slot, 1)
            dve.wait_ge(r_mm, 3 * l + 3)
            link(V.tensor_copy(sti[:, 0:2 * NTB], ps[:, 5, 0:2 * NTB]))
            fence()

            m, mx = moe[2 * l], moe[2 * l + 1]
            xgt_step(l, m, 0, 0, None)
            hb_after(m, l)
            fence()

        def hb_after(m, l):
            mx = moe[2 * l + 1]
            hb_step(m, 0)
            xgt_step(l, m, 1, 1, None)
            with dve.Fori(0, NPB // 2 - 1) as j:
                hb_step(m, 2 * j + 1)
                xgt_step(l, m, 2 * j + 2, 0, 2 * j + 1)
                hb_step(m, 2 * j + 2)
                xgt_step(l, m, 2 * j + 3, 1, 2 * j + 2)
            hb_step(m, NPB - 1)
            n_pairs = dve.value_load(sti[0:1, XN:XN + 1], min_val=0, max_val=NXP)
            with dve.Fori(0, NXP) as j:
                with dve.If(n_pairs > j):
                    xgt_step(l, mx, j, 0, j)
                    hb_step(mx, j)
            for t in range(NT):
                r = rows(t)
                dve.wait_ge(y_back[t % 2], 16 * (l * (3 - t % 2) + t // 2 + 1))
                link(V.scalar_tensor_tensor(xt[0:r, t], y01[0:r, t % 2, 0], wts[0:r, 0, t:t + 1], xt[0:r, t],
                                            ALU.mult, ALU.add))
                V.scalar_tensor_tensor(xt[0:r, t], y01[0:r, t % 2, 1], wts[0:r, 1, t:t + 1], xt[0:r, t],
                                       ALU.mult, ALU.add).then_inc(y_used, 1)

        layer_ffn(0)
        norm(2)
        fence()

        dve.wait_ge(state_in, 16 * KC)

        def gate(ch):
            bank = 4 * (ch % 2)
            ba = PR("b_pw1")[:, ch:ch + 1]
            dve.wait_ge(pw_sig, ch + 1)
            S(V.scalar_tensor_tensor(u_ext[:, ch, CK - 1:CK - 1 + HALF], ps[:, bank, 0:HALF], ba,
                                     sig[:, ch % 2, 0:HALF], ALU.add, ALU.mult))
            rest = TP - HALF
            S(V.scalar_tensor_tensor(u_ext[:, ch, CK - 1 + HALF:CK - 1 + TP], ps[:, bank + 1, 0:rest], ba,
                                     sig[:, ch % 2, HALF:TP], ALU.add, ALU.mult))
            V.scalar_tensor_tensor(us[:, ch, :, CK - 1:], ps[:, bank + 1, rest:HALF].rearrange("p (b q) -> p b q", b=NB),
                                   ba, sig[:, ch % 2, TP:T].rearrange("p (b q) -> p b q", b=NB),
                                   ALU.add, ALU.mult).then_inc(glu, 1)

        def taps(ch):
            dve.wait_ge(glu, ch + 1)
            S.done()
            for j in range(CK):
                for o, i in ((cc[:, ch, 0:TP], u_ext[:, ch, j:j + TP]),
                             (cc[:, ch, TP:T].rearrange("p (b q) -> p b q", b=NB), us[:, ch, :, j:j + NQ])):
                    if j == 0:
                        S(V.tensor_scalar(o, i, wdw[:, ch, 0:1], PR("b_dw")[:, ch:ch + 1], ALU.mult, ALU.add))
                    else:
                        dve.wait_ge(dve_step, S.n - 1)
                        S(V.scalar_tensor_tensor(o, i, wdw[:, ch, j:j + 1], o, ALU.mult, ALU.add))

        gate(0)
        taps(0)
        gated = 1
        for ch in range(1, KC - 2):
            for _ in range(2):
                if gated < KC:
                    gate(gated)
                    gated += 1
            taps(ch)
        fence()

        dve.wait_ge(ln_sums, 1)
        mean, inv = mr[:, 0, :], mr[:, 1, :]
        halves = "p (h n) -> p h n"
        link(V.tensor_scalar(mean.rearrange(halves, h=2), ps[:, 0:2, 0:HALF], 1.0 / D, None, ALU.mult))
        V.tensor_tensor(cc, cc, mean.unsqueeze(1).broadcast_to((P, KC, T)), ALU.subtract).then_inc(ln_steps, 1)
        dve.wait_ge(ln_sums, KC + 1)
        V.tensor_scalar(inv.rearrange(halves, h=2), ps[:, 2:4, 0:HALF], 1.0 / D, EPS, ALU.mult, ALU.add).then_inc(ln_steps, 1)
        dve.wait_ge(ln_squares, KC + 1)
        link(V.reciprocal(inv, inv))
        dve.wait_ge(ln_steps, 1)
        for ch in range(KC):
            V.tensor_tensor(cc[:, ch], cc[:, ch], inv, ALU.mult).then_inc(ln_steps, 1)
        fence()
        residual(1)
        fence()
        layer_ffn(1)

        dve.wait_ge(norm_sq, 5)
        rstd(st[:, 5:10], st[:, 0:5], D)
        dve.wait_ge(x_in, 48)
        for t in range(NT):
            r = rows(t)
            if t >= 2:
                dve.wait_ge(rows_out2[t % 2], 16 * (2 * (3 - t % 2) + t // 2))
            V.scalar_tensor_tensor(xn[0:r, t % 2, :], xt[0:r, t, :], st[0:r, 5 + t:6 + t], gf[0:r, :],
                                   ALU.mult, ALU.mult).then_inc(norm_rows, 1)

    @block.tensor
    def _(pe):
        fence = Fence(pe, "pe")
        mm = nc.tensor.matmul

        def turn(o, i, n=P):
            return nc.tensor.transpose(o, i, ident[0:n, 0:n])

        def norm(u, turned=None):
            for t in range(NT):
                r = rows(t)
                pe.wait_ge(norm_rows, NT * u + t + 1)
                if t >= 2:
                    pe.wait_ge(norm_ev, NT * u + t - 1)
                for k in range(KC):
                    ins = turn(ps[:, 2 * (t % 2) + k // 4, (k % 4) * P:(k % 4) * P + r],
                               xn[0:r, t % 2, k * P:(k + 1) * P], r)
                ins.then_inc(norm_tr, 1)
                if turned and t:
                    turned(t - 1)
            if turned:
                turned(NT - 1)

        pe.wait_ge(consts_in, 48)
        pe.wait_ge(lam_ready, 1)
        mm(ps[:, 7, 0:2], ones, st[:, 22:24], start=True, stop=True).then_inc(lam_mm, 1)
        norm(0)
        fence()

        def z_turn(n, t, k):
            r = rows(t)
            pe.wait_ge(z_rope, k + 1)
            if k > 1:
                pe.wait_ge(z_tev, k - 1)
            for h in range(4):
                ins = turn(ps[:, k % 2, h * P:h * P + r], zrow[0:r, k % 4, h * P:(h + 1) * P], r)
            ins.then_inc(z_tr, 1)

        prev, i_z = [], 0
        for n in range(6):
            pe.wait_ge(loaded[n], 16)
            for t in range(NT):
                r = rows(t)
                if i_z > 3:
                    pe.wait_ge(z_copy, i_z - 3)
                for k in range(KC):
                    ins = mm(ps[0:r, 4 + i_z % 4, :], act_t[:, k, t * P:t * P + r], slot(n, 8)[:, k, :],
                             start=(k == 0), stop=(k == KC - 1))
                ins.then_inc(z_mm, 1)
                i_z += 1
                if prev:
                    z_turn(*prev.pop())
                if n in qtab:
                    prev.append((n, t, qtab[n] * NT + t))
        if prev:
            z_turn(*prev.pop())
        fence()

        for s in range(NI + 3):
            if s < NI:
                qt, kind, c = ITEMS[s]
                n = (qt + 1) * P
                if 2 * (s - 1) > 0:
                    pe.wait_ge(a_exp, 2 * (s - 1))
                for j in range(2):
                    p = slice(64 * j, 64 * j + 64)
                    ins = mm(ps[:, 2 * (s % 2) + j, 0:n], qT[kind][p, c, qt * P:(qt + 1) * P],
                             kT[kind][p, c, 0:n], start=True, stop=True)
                ins.then_inc(a_s, 1)
            m = s - 2
            if 0 <= m < NI:
                qt, kind, c = ITEMS[m]
                pe.wait_ge(a_ptev, m + 1)
                if m > 0:
                    pe.wait_ge(a_row, m)
                nj = 2 if kind else 1
                for j in range(nj):
                    w = P // nj
                    for kb in range(qt + 1):
                        ins = mm(ps[:, 6, j * w:(j + 1) * w], PTsb[:, m % 2, j, kb * P:(kb + 1) * P],
                                 vP[kind][:, kb, c * P + j * w:c * P + (j + 1) * w],
                                 start=(kb == 0), stop=(kb == qt))
                ins.then_inc(a_o, 1)
            m = s - 1
            if 0 <= m < NI:
                qt, kind, c = ITEMS[m]
                pe.wait_ge(a_p, m + 1)
                if m > 0:
                    pe.wait_ge(a_ptev, m)
                for j in range(2 if kind else 1):
                    for kb in range(qt + 1):
                        ins = turn(ps[:, 4 + j, kb * P:(kb + 1) * P], Ex[:, m % 2, j, kb * P:(kb + 1) * P])
                ins.then_inc(a_t, 1)
            m = s - 3
            if 0 <= m < NI and ITEMS[m][1] == 1:
                qt, kind, c = ITEMS[m]
                done = turned_before(m)
                pe.wait_ge(a_row, m + 1)
                if done:
                    pe.wait_ge(a_cat, done)
                turn(ps[:, 7, 0:P], orow[:, c % 2, :]).then_inc(a_ot, 1)
                if c == 3:
                    pe.wait_ge(a_norm, qt + 1)
                    pe.wait_ge(a_cat, done + 1)
                    for h in range(4):
                        ins = turn(ps[:, 7, h * P:(h + 1) * P], orow4[:, h, :])
                    ins.then_inc(a_ot, 1)
        fence()
        fence()

        with pe.Fori(0, NB) as b:
            def turn_keys(g):
                s, first, nb, _ = GROUPS[g]
                if g in (1, 3, 5):
                    pe.wait_ge(loaded[s], b * PER_BATCH[s] + 16 + PER_BATCH[s])
                if g == 7:
                    pe.wait_ge(aux_in[0], b * 16 + 16)
                for c in range(4):
                    u = 4 * (g - 1) + c
                    pe.wait_ge((te_act, te_dve)[c % 2], b * 14 + u // 2 + 1)
                    for i in range(nb):
                        blk = aux[:, i, c * P:(c + 1) * P] if s is None else slot(s, 8)[:, first + i, c * P:(c + 1) * P]
                        ins = turn(ps[:, c % 2, i * P:(i + 1) * P], blk)
                    ins.then_inc(t_done, 1)

            def scores(g):
                bank = 2 + g % 2
                if g in (0, 1):
                    pe.wait_ge(sw_ev, b * 4 + 1)
                elif g in (2, 7):
                    pe.wait_ge(sw_ev, (b * 4 + (1 if g == 2 else 2)) + 1)
                else:
                    pe.wait_ge(sd_ev, b * 4 + g - 2)
                if g == 0:
                    pe.wait_ge(q_ready, b + 1)
                    for w in range(2):
                        for c in range(4):
                            ins = mm(ps[32 * c:32 * c + 32, bank, w * TS:(w + 1) * TS], Qcur[:, w, c, :],
                                     kS[w][:, c, :], start=True, stop=True)
                else:
                    pe.wait_ge(te_act, b * 14 + 2 * g + 1)
                    pe.wait_ge(te_dve, b * 14 + 2 * g + 1)
                    n = GROUPS[g][2] * P
                    for c in range(4):
                        ins = mm(ps[32 * c:32 * c + 32, bank, 0:n], Qcur[:, int(g > 4), c, :],
                                 KTs[:, 4 * (g % 2) + c, 0:n], start=True, stop=True)
                ins.then_inc(s_mm, 1)

            def turn_probs(k):
                w, blocks = CHUNKS[k]
                if k in (0, 5):
                    pe.wait_ge(exp_done, b * 2 + w + 1)
                    pe.sem_inc(waited)
                if k % 2:
                    pe.wait_ge(ptev_act, b * 5 + (k - 1) // 2 + 1)
                    pe.sem_inc(waited)
                else:
                    pe.wait_ge(ptev_dve, b * 4 + k // 2 + 1)
                    pe.sem_inc(waited)
                for i, blk in enumerate(blocks):
                    src, new = (S_w, 10) if w else (S_d, 16)
                    n = TS if blk == new else P
                    ins = turn(ps[0:n, 4 + k % 2, i * P:(i + 1) * P], src[:, blk * P:blk * P + n])
                ins.then_inc(pt_done, 1)

            def products(k):
                w, blocks = CHUNKS[k]
                if k % 2:
                    pe.wait_ge(ptev_act, (b * 5 + ((k - 1) // 2 + 1 if k < 7 else 5)) + 1)
                    pe.sem_inc(waited)
                else:
                    pe.wait_ge(ptev_dve, b * 4 + k // 2 + 2)
                    pe.sem_inc(waited)
                for s, at in ((2, 0), (3, 2), (5, 5)):
                    if k == at:
                        pe.wait_ge(loaded[s], b * PER_BATCH[s] + 16 + PER_BATCH[s])
                if k == 7:
                    pe.wait_ge(aux_in[1], b * 16 + 16)
                if k in (0, 5):
                    pe.wait_ge(o_ev, b * 2 + 1)
                for blk in blocks:
                    r = P
                    if w:
                        if blk < 8:
                            v = slot(5, 8)[:, blk, :]
                        elif blk < 10:
                            v = aux[:, 2 + blk - 8, :]
                        else:
                            v, r = vS[1][0:TS], TS
                    elif blk < 16:
                        v = slot(2 + blk // 8, 8)[:, blk % 8, :]
                    else:
                        v, r = vS[0][0:TS], TS
                    pt = PT_w if w else PT_d
                    for c in range(4):
                        ins = mm(ps[32 * c:32 * c + 32, 6 + w, 0:P], pt[0:r, blk, 32 * c:32 * c + 32],
                                 v[:, c * P:(c + 1) * P], start=(blk == 0), stop=(blk == (10 if w else 16)))
                ins.then_inc(pv_done, 1)

            turn_keys(1); scores(0)
            for g in range(2, 8):
                turn_keys(g)
                scores(g - 1)
            scores(7)
            turn_probs(0)
            for k in range(8):
                if k < 7:
                    turn_probs(k + 1)
                products(k)
        fence()

        for i in range(2):
            ins = mm(ps[0:32, i, :], C("pair"), O_all[0][:, 4 * i:4 * i + 4, :].rearrange("p b d -> p (b d)"),
                     start=True, stop=True)
        ins.then_inc(f_mm, 1)
        for b in range(NB):
            turn(ps[:, 3 + b // 4, (b % 4) * P:(b % 4 + 1) * P], O_all[1][:, b, :])
        pe.wait_ge(f_ev, 2)
        for b in range(NB):
            ins = turn(ps[:, 2, 32 * b:32 * b + 32], comb[0:32, b, :], 32)
        ins.then_inc(f_mm, 1)
        fence()

        def project(u, src, done):
            for i in range(2 * NT):
                n, t = divmod(i, NT)
                r = rows(t)
                if t == 0:
                    pe.wait_ge(loaded[n], done[n])
                if i >= 4:
                    pe.wait_ge(p_ev, u * 2 * NT + i - 3)
                if u:
                    mm(ps[0:r, i % 4, :], ones[0:1, 0:r], brow[:, n * 512:(n + 1) * 512], start=True, stop=False)
                for k in range(KC):
                    ins = mm(ps[0:r, i % 4, :], src[:, k, t * P:t * P + r], slot(n, 8)[:, k, :],
                             start=(k == 0 and not u), stop=(k == KC - 1))
                ins.then_inc(p_mm, 1)

        project(0, act_t, [AFTER_BATCH[s] + 16 for s in range(2)])
        fence()

        def xt_step(m, n, par_, gathered):
            pe.wait_ge(m[f"gathered{par_}"], gathered)
            pe.wait_ge(m["xgt"], n + 1)
            for k in range(KC):
                ins = turn(ps[:, 2 + k // 4, (k % 4) * P:(k % 4 + 1) * P], Xg[:, par_, k * P:(k + 1) * P])
            ins.then_inc(m["xt"], 1)

        def gu_step(m, n, par_, weights):
            pe.wait_ge(m["xgt"], n + 2)
            for i, (name, used) in enumerate((("g", "silu"), ("u", "hb"))):
                pe.wait_ge(m[used], n + 1)
                weights(i)
                for k in range(KC):
                    for w in range(2):
                        half = slice(w * HB, (w + 1) * HB)
                        ins = mm(ps[half, i, :], XgT[:, par_, k, half], slot(eslots(w)[i], 8)[:, k, :],
                                 start=(k == 0), stop=(k == KC - 1))
                ins.then_inc(m[name], 1)

        def down_step(m, n, weights):
            pe.wait_ge(m["hb"], n + 2)
            pe.wait_ge(m["hbt"], n + 1)
            for k in range(4):
                ins = turn(ps[:, 4, k * P:(k + 1) * P], hb[:, k * P:(k + 1) * P])
            ins.then_inc(m["ht"], 1)
            weights(2)
            pe.wait_ge(m["hbt"], n + 2)
            for h in range(2):
                pe.wait_ge(m["yev"], 2 * n + 1)
                for k in range(4):
                    for w in range(2):
                        half = slice(w * HB, (w + 1) * HB)
                        ins = mm(ps[half, 5 + h, :], hbT[:, k, half],
                                 slot(eslots(w)[2], 4)[:, k, h * 512:(h + 1) * 512], start=(k == 0), stop=(k == 3))
                ins.then_inc(m["y"], 1)

        def layer_ffn(l):
            def logits(t):
                r = rows(t)
                pe.wait_ge(norm_ev, NT * (1 + 2 * l) + t + 1)
                for k in range(KC):
                    ins = mm(ps[0:r, 7, t * 36:(t + 1) * 36], act_t[:, k, t * P:t * P + r], router[:, l, k, :],
                             start=(k == 0), stop=(k == KC - 1))
                if t == NT - 1:
                    ins.then_inc(r_mm, 1)

            norm(1 + 2 * l, logits)
            fence()
            pe.wait_ge(r_ev, 3 * l + 3)
            for t in range(NT):
                for i in range(t + 1):
                    mm(ps[:, 6, t * NE:(t + 1) * NE], C("before") if i == t else ones, both[:, i, :],
                       start=(i == 0), stop=(i == t))
            for i in range(NT):
                ins = mm(ps[:, 6, 160:192], ones, both[:, i, :], start=(i == 0), stop=(i == NT - 1))
            ins.then_inc(r_mm, 1)
            pe.wait_ge(table_io, 32 + (l + 1) * 16 * 11)
            for i in range(2):
                ins = turn(ps[:, 5, NTB * i:NTB * (i + 1)], tab[:, :, i], NTB)
            ins.then_inc(r_mm, 1)
            fence()

            m, mx = moe[2 * l], moe[2 * l + 1]

            def weights(turns):
                def w(kind):
                    for par_ in range(2):
                        s = eslots(par_)[kind]
                        pe.wait_ge(loaded[s], turns * 16 + moe_base(l, s))
                return w

            xt_step(m, 0, 0, 16)
            with pe.Fori(0, NPB // 2 - 1) as j:
                gu_step(m, 2 * j, 0, weights(2 * j + 1))
                xt_step(m, 2 * j + 1, 1, j * 16 + 16)
                down_step(m, 2 * j, weights(2 * j + 1))
                gu_step(m, 2 * j + 1, 1, weights(2 * j + 2))
                xt_step(m, 2 * j + 2, 0, j * 16 + 32)
                down_step(m, 2 * j + 1, weights(2 * j + 2))
            gu_step(m, NPB - 2, 0, weights(NPB - 1))
            xt_step(m, NPB - 1, 1, 16 * NPB // 2)
            down_step(m, NPB - 2, weights(NPB - 1))
            gu_step(m, NPB - 1, 1, weights(NPB))
            down_step(m, NPB - 1, weights(NPB))
            pe.wait_ge(m["yev"], 2 * NPB + 1)
            n_pairs = pe.value_load(sti[0:1, XN:XN + 1], min_val=0, max_val=NXP)
            with pe.Fori(0, NXP // 2) as j:
                for par_ in range(2):
                    with pe.If(n_pairs > 2 * j + par_):
                        def x_weights(kind):
                            pe.wait_ge(x_loaded[l][kind], j * 64 + (par_ + 1) * 32)
                        xt_step(mx, 2 * j + par_, par_, j * 16 + 16)
                        gu_step(mx, 2 * j + par_, 0, x_weights)
                        down_step(mx, 2 * j + par_, x_weights)
            fence()

        layer_ffn(0)
        norm(2)
        fence()

        for ch in range(KC):
            first = 2 + 2 * (ch // 4)
            if ch % 4 == 0:
                for s in (first, first + 1):
                    pe.wait_ge(loaded[s], moe_base(1, s))
            if ch > 1:
                pe.wait_ge(glu, ch - 1)
            for i in range(2):
                for h in range(2):
                    for k in range(KC):
                        ins = mm(ps[:, 4 * (ch % 2) + 2 * i + h, 0:HALF],
                                 slot(first + i, 8)[:, k, (ch % 4) * P:(ch % 4 + 1) * P],
                                 act_t[:, k, h * HALF:(h + 1) * HALF], start=(k == 0), stop=(k == KC - 1))
            ins.then_inc(pw_mm, 1)
        def diagonal_taps(i):
            c = PE_CH[i]
            pe.wait_ge(diagonals, i + 1)
            pe.wait_ge(glu, c + 1)
            for j in range(CK):
                tap = slot(2 + i, 32)[:, j, :]
                mm(ps[:, 2 * i, :], tap, u_ext[:, c, j:j + TP], start=(j == 0), stop=(j == CK - 1))
                ins = mm(ps[:, 2 * i + 1, 0:TS].rearrange("p (b q) -> p b q", b=NB), tap, us[:, c, :, j:j + NQ],
                         start=(j == 0), stop=(j == CK - 1))
            ins.then_inc(pw_mm, 1)

        diagonal_taps(0)
        pe.wait_ge(glu, KC)
        last = TP
        for ch in range(KC):
            c0 = (ch % 4) * P
            turn(ps[0:CK - 1, 4 + ch // 4, c0:c0 + P], u_ext[:, ch, last:last + CK - 1])
            if ch == 0:
                pe.wait_ge(cv_new, 1)
            ins = turn(ps[0:TS, 6 + ch // 4, c0:c0 + P], act_t[:, ch, 0:TS])
        ins.then_inc(pw_mm, 1)
        diagonal_taps(1)
        fence()

        for h in range(2):
            for ch in range(KC):
                ins = mm(ps[:, h, 0:HALF], ones, cc[:, ch, h * HALF:(h + 1) * HALF], start=(ch == 0), stop=(ch == KC - 1))
        ins.then_inc(ln_sums, 1)
        for ch in range(KC):
            pe.wait_ge(ln_squares, ch + 1)
            for h in range(2):
                ins = mm(ps[:, 2 + h, 0:HALF], ones, sig[:, ch % 2, h * HALF:(h + 1) * HALF],
                         start=(ch == 0), stop=(ch == KC - 1))
            ins.then_inc(ln_sums, 1)
        fence()
        pe.wait_ge(state_in, 16 * KC + 16)
        project(1, cc, [moe_base(1, s) for s in range(2)])
        fence()
        layer_ffn(1)

    @block.gpsimd
    def _(pool):
        G = Steps(pool, pool_step)
        fence = Fence(pool, "pool")
        IDX = bass.IndirectOffsetOnAxis

        def load_x(src_p, src_s):
            pool.dma_start(xt[:, 0:4, :], src_p.rearrange("(t p) d -> p t d", p=P)).then_inc(x_in, 16)
            pool.dma_start(xt[0:TS, 4, :], src_s).then_inc(x_in, 16)

        for q in with_lead:
            pool.sem_inc(q)
        far = B(0, 256)[0:NPB + NXP]
        G(nc.gpsimd.memset(far, FAR))
        G.done()
        for l in range(2):
            pool.dma_start(table[l].rearrange("(b s) c -> b (s c)", s=P), far).then_inc(table_io, 16)
        pool.wait_ge(table_io, 32)
        fence()

        outs = {1: (nkd_p, nkd_s), 2: (nvd_p, nvd_s), 4: (nwk_p, nwk_s), 5: (nwv_p, nwv_s)}
        n_v = 0
        for n in range(6):
            for t in range(NT):
                if n not in outs:
                    continue
                dst = outs[n][0][t * P:(t + 1) * P] if t < 4 else outs[n][1]
                if t == 4 and n > 3:
                    dst = dst[:, PAST - NQ:PAST, :]
                if n in qtab:
                    k = qtab[n] * NT + t
                    pool.wait_ge(z_rope, k + 1)
                    src = zrow[0:rows(t), k % 4, :]
                    pool.dma_start(dst, src).then_inc(z_out[k % 4], 16)
                else:
                    pool.wait_ge(z_copy, n * NT + t + 1)
                    src = vP[n // 4][:, t, :] if t < 4 else vS[n // 4][0:TS, :]
                    pool.dma_start(dst, src).then_inc(out_done, 16)
                    n_v += 1
        for i in range(4):
            pool.wait_ge(z_out[i], 16 * stores_before(20 + i))
        pool.wait_ge(out_done, 16 * n_v)
        for _ in range(5):
            fence()
        load_x(x_prompt, x_sample)
        fence()

        def layer_ffn(l):
            for t in range(NT):
                r = rows(t)
                pool.wait_ge(norm_rows, NT * (1 + 2 * l) + t + 1)
                pool.dma_start(h_rows[l][t * P:t * P + r], xn[0:r, t % 2, :]).then_inc(rows_out2[t % 2], 16)
            for i in range(2):
                pool.wait_ge(rows_out2[i], 16 * (3 - i) * (l + 1))
            fence()
            G(nc.gpsimd.memset(Xg, 0.0))
            G.done()
            pool.wait_ge(r_slot, 2 * l + 1)
            for s in range(2):
                for t in range(NT):
                    r = rows(t)
                    pool.indirect_dma_start(table[l], IDX(slotI[0:r, s * NT + t:s * NT + t + 1], 0),
                                            codes[0:r, s, t, :], None,
                                            bounds_check=(NPB + NXP) * P - 1, oob_is_err=False).then_inc(table_io, 16)
            pool.wait_ge(table_io, 32 + l * 16 * 11 + 160)
            pool.dma_start(tab.rearrange("b s c -> b (s c)"),
                           table[l].rearrange("(b s) c -> b (s c)", s=P)).then_inc(table_io, 16)
            fence()

            m, mx = moe[2 * l], moe[2 * l + 1]

            def gather_dma(mm_, par_):
                pool.indirect_dma_start(Xg[:, par_, :], None, h_rows[l], IDX(tokS[:, par_:par_ + 1], 0),
                                        bounds_check=T - 1, oob_is_err=False).then_inc(mm_[f"gathered{par_}"], 16)

            def scatter_dma(mm_, par_):
                pool.indirect_dma_start(y_rows[l], IDX(codeS[:, par_:par_ + 1], 0), Y[:, par_, :], None,
                                        bounds_check=2 * T - 1, oob_is_err=False).then_inc(mm_[f"scattered{par_}"], 16)

            def do_gather(mm_, xt_needed, par_, block_, ready):
                if xt_needed is not None:
                    pool.wait_ge(mm_["xt"], xt_needed)
                    pool.sem_inc(waited)
                pool.tensor_copy(tokS[:, par_:par_ + 1], tokI[:, block_]).then_inc(tok_ready, 1)
                pool.wait_ge(tok_ready, ready)
                pool.sem_inc(waited)
                gather_dma(mm_, par_)

            def do_scatter(mm_, n, par_, block_, used, ready):
                pool.wait_ge(mm_["yev"], 2 * n + 3)
                pool.sem_inc(waited)
                if used is not None:
                    pool.wait_ge(mm_[f"scattered{par_}"], used)
                    pool.sem_inc(waited)
                pool.tensor_copy(codeS[:, par_:par_ + 1], codeI[:, block_]).then_inc(code_ready, 1)
                pool.wait_ge(code_ready, ready)
                pool.sem_inc(waited)
                scatter_dma(mm_, par_)

            base = l * NPB
            for par_ in range(2):
                do_gather(m, None, par_, slice(par_, par_ + 1), base + par_ + 1)
            for par_ in range(2):
                do_gather(m, par_ + 1, par_, slice(2 + par_, 3 + par_), base + 3 + par_)
                do_scatter(m, par_, par_, slice(par_, par_ + 1), None, base + 1 + par_)
            with pool.Fori(1, NPB // 2 - 1) as j:
                for par_ in range(2):
                    do_gather(m, 2 * j + par_ + 1, par_, bass.ds(2 * j + 2 + par_, 1), 2 * j + (base + 3 + par_))
                    do_scatter(m, 2 * j + par_, par_, bass.ds(2 * j + par_, 1), j * 16, 2 * j + (base + 1 + par_))
            n_pairs = pool.value_load(sti[0:1, XN:XN + 1], min_val=0, max_val=NXP)

            def extra_gather(i, par_, block_, copies):
                pool.tensor_copy(tokS[:, par_:par_ + 1], sti[:, block_]).then_inc(x_tok[l], 1)
                pool.wait_ge(x_tok[l], copies)
                pool.sem_inc(waited)
                gather_dma(mx, par_)

            for par_ in range(2):
                n = NPB - 2 + par_
                with pool.If(n_pairs > par_):
                    pool.wait_ge(m["xt"], n + 1)
                    extra_gather(par_, par_, slice(NPB + par_, NPB + par_ + 1), par_ + 1)
                do_scatter(m, n, par_, slice(n, n + 1), (NPB // 2 - 1) * 16, base + n + 1)
            for par_ in range(2):
                pool.wait_ge(m[f"scattered{par_}"], 16 * NPB // 2)
                pool.sem_inc(waited)

            def extra_scatter(i, block_):
                pool.wait_ge(mx["yev"], 2 * i + 3)
                pool.sem_inc(waited)
                pool.tensor_copy(codeS[:, 0:1], sti[:, bass.ds(block_ + NTB, 1)]).then_inc(x_stored[l], 1)
                pool.wait_ge(x_stored[l], 2 * i + 2)
                pool.sem_inc(waited)
                scatter_dma(mx, 0)

            with pool.If(n_pairs > 0):
                extra_scatter(0, NPB)
                with pool.If(n_pairs > 2):
                    pool.wait_ge(mx["xt"], 1)
                    extra_gather(2, 0, slice(NPB + 2, NPB + 3), 3)
                pool.wait_ge(mx["scattered0"], 16)
                pool.sem_inc(x_stored[l])
            with pool.If(n_pairs > 1):
                with pool.Fori(0, NXP // 2) as j:
                    for i_, par_ in ((2 * j + 1, 1), (2 * j + 2, 0)):
                        with pool.If(n_pairs > i_):
                            extra_scatter(i_, i_ + NPB)
                        with pool.If(n_pairs > i_ + 2):
                            pool.wait_ge(mx["xt"], i_ + 1)
                            pool.sem_inc(waited)
                            extra_gather(i_ + 2, par_, bass.ds(i_ + NPB + 2, 1), i_ + 3)
                        with pool.If(n_pairs > i_):
                            pool.wait_ge(mx["scattered0"], 16 * i_ + 16)
                            pool.sem_inc(x_stored[l])
            for t in range(NT):
                r = rows(t)
                if t >= 2:
                    pool.wait_ge(y_used, NT * l + t - 1)
                pool.dma_start(y01[0:r, t % 2], y_rows[l][2 * P * t:2 * P * t + 2 * r].rearrange("(p s) d -> p s d", s=2)
                               ).then_inc(y_back[t % 2], 16)
            fence()

        layer_ffn(0)
        fence()
        G(nc.gpsimd.memset(u_ext[:, :, 0:CK - 1], 0.0))
        G.done()
        for ch in range(KC):
            pool.dma_start(u_ext[:, ch, CK - 1 + TP:].rearrange("p (b w) -> p b w", b=NB)[:, :, 0:CK - 1],
                           st_cols[ch]).then_inc(state_in, 16)
        pool.wait_ge(cv_ev, 2)
        pool.dma_start(ncv_p, crow_p).then_inc(out_done, 16)
        pool.dma_start(ncv_s[:, CK - 1 - NQ:, :], crow_s).then_inc(out_done, 16)
        pool.wait_ge(out_done, 16 * (n_v + 2))
        fence()
        pool.dma_start(brow, vecs[0:1, :]).then_inc(state_in, 16)
        fence()
        fence()
        layer_ffn(1)
        pool.dma_start(gf, vecs[1:2, :].broadcast_to((P, D))).then_inc(x_in, 16)
        for t in range(NT):
            r = rows(t)
            pool.wait_ge(norm_rows, 4 * NT + t + 1)
            dst = y_p[t * P:(t + 1) * P] if t < 4 else y_s
            pool.dma_start(dst, xn[0:r, t % 2, :]).then_inc(rows_out2[t % 2], 16)
        for i in range(2):
            pool.wait_ge(rows_out2[i], 16 * (3 - i) * 3)

    ctx.close()


_OUTS = [(1, 512, 1024), (8, 8, 1024), (1, 1, 512, 4, 128), (1, 1, 512, 4, 128), (1, 8, 8, 4, 128), (1, 8, 8, 4, 128),
         (1, 1, 512, 8, 64), (1, 1, 512, 8, 64), (1, 8, 2048, 8, 64), (1, 8, 2048, 8, 64), (1, 1, 30, 1024), (1, 8, 30, 1024)]
_VIEWS = [(512, 1024), (64, 1024), (512, 512), (512, 512), (64, 512), (64, 512),
          (512, 512), (512, 512), (8, 2048, 512), (8, 2048, 512), (30, 1024), (8, 30, 1024)]


def kernel(**inputs):
    import numpy as _np
    import concourse.bacc as _bacc
    from concourse import mybir as _mybir
    from concourse.bass_utils import run_bass_kernel_spmd as _run

    a = {k: _np.asarray(v) for k, v in inputs.items()}

    def cols(v, n):
        return v.reshape(n, P).T

    def pad(v):
        return _np.concatenate([v.reshape(-1), _np.zeros(P - HD, v.dtype)]).reshape(P, 1)

    routers = []
    for l in range(2):
        w = _np.concatenate([a["w_router_group"][l], a["w_router_expert"][l].transpose(1, 0, 2).reshape(D, NE)], 1)
        routers.append(w.reshape(KC, P, 36).transpose(1, 0, 2).reshape(P, -1))
    params = _np.concatenate(
        [cols(a["norm_mix"][0], KC), cols(a["norm_ffn"][0], KC), cols(a["norm_mix"][1], KC), cols(a["norm_ffn"][1], KC),
         a["subln_gain"].reshape(P, 1),
         a["w_dw"][0].T.reshape(KC, P, CK).transpose(1, 0, 2).reshape(P, -1),
         cols(a["b_dw"][0], KC), cols(a["ln_conv_gain"][0], KC), cols(a["ln_conv_bias"][0], KC),
         cols(a["b_pw1"][0], 16), *routers,
         pad(a["lambda_q1"]), pad(a["lambda_k1"]), pad(a["lambda_q2"]), pad(a["lambda_k2"])], 1)
    st = a["state_conv"][0]
    arrays = [
        a["x_prompt"][0], a["x_sample"].reshape(TS, D),
        a["cache_k_diff"][0].reshape(-1, PAGE, 512), a["cache_v_diff"][0].reshape(-1, PAGE, 512),
        a["cache_win_k"][0].reshape(NB, PAST, 512), a["cache_win_v"][0].reshape(NB, PAST, 512),
        st, st.transpose(2, 0, 1).reshape(KC, P, NB, CK - 1),
        a["page_table"].reshape(1, -1), a["w_in_attn"][0], a["w_out_attn"][0], a["w_pw1"][0], a["w_pw2"][0],
        a["w_exp_gate"].reshape(-1, D, F), a["w_exp_up"].reshape(-1, D, F), a["w_exp_down"].reshape(-1, F, D),
        params, _np.concatenate(list(constants().values()), 1),
        _np.concatenate([a["b_pw2"], a["norm_final"].reshape(1, D)], 0)]
    nc = _bacc.Bacc("TRN2", target_bir_lowering=False, num_devices=1)
    given, args = {}, []
    for i, v in enumerate(arrays):
        v = _np.ascontiguousarray(v)
        given[f"in_{i}"] = v
        args.append(nc.dram_tensor(f"in_{i}", v.shape, _mybir.dt.from_np(v.dtype), kind="ExternalInput").ap())
    for i, shape in enumerate(_VIEWS):
        args.append(nc.dram_tensor(f"out_{i}", shape, _mybir.dt.float32, kind="ExternalOutput").ap())
    build(nc, *args)
    r = _run(nc, [given], core_ids=[0])
    return tuple(r.results[0][f"out_{i}"].reshape(s) for i, s in enumerate(_OUTS))
```
